# Optimizing a Trainium2 kernel written in Bass

```python
import jax, jax.numpy as jnp
from jax import lax
import numpy as np

D_MODEL = 1024
BATCH = 1
SEQ = 512
DEPTH = 1

N_MEM = 256
POOL_WIDTH = D_MODEL
POOL_WINDOWS = (2, 4, 8, 16)
POOL_GROUPS = len(POOL_WINDOWS)
POOL_GROUP_DIM = POOL_WIDTH // POOL_GROUPS
LRU_WIDTH = D_MODEL
LRU_HEADS = 8
LRU_HEAD_DIM = LRU_WIDTH // LRU_HEADS
LRU_CONV = 4
LRU_C = 8.0
SCONV_WIDTH = D_MODEL
SCONV_K = 3
N_BRANCH = 3
SPLIT_POINTS = (POOL_WIDTH,
                POOL_WIDTH + LRU_WIDTH,
                POOL_WIDTH + LRU_WIDTH + SCONV_WIDTH,
                POOL_WIDTH + LRU_WIDTH + 2 * SCONV_WIDTH,
                POOL_WIDTH + LRU_WIDTH + 3 * SCONV_WIDTH)
IN_COLS = POOL_WIDTH + LRU_WIDTH + 3 * SCONV_WIDTH + N_BRANCH * D_MODEL
X_HEADS = 4
X_HEAD_DIM = D_MODEL // X_HEADS
D_FF = -(-8 * D_MODEL // (3 * 256)) * 256
ALPHA = (2 * DEPTH) ** 0.25
BETA = (8 * DEPTH) ** -0.25
LN_EPS = 1e-5

kernel_name = "hybrid_pool_rglru_shortconv_deepnorm"

def layer_norm(x, g, b):
    xf = x.astype(jnp.float32)
    mu = jnp.mean(xf, axis=-1, keepdims=True)
    var = jnp.mean(jnp.square(xf - mu), axis=-1, keepdims=True)
    y = (xf - mu) * lax.rsqrt(var + LN_EPS)
    return (y * g.astype(jnp.float32) + b.astype(jnp.float32)).astype(x.dtype)

def causal_depthwise_conv(u, w):
    k, c = w.shape
    return lax.conv_general_dilated(
        u, w[:, None, :].astype(u.dtype), window_strides=(1,),
        padding=((k - 1, 0),), dimension_numbers=("NWC", "WIO", "NWC"),
        feature_group_count=c)

def multiscale_pool(u, pool_w, pool_scale):
    bsz, s, _ = u.shape
    uf = u.astype(jnp.float32)
    cs = jnp.cumsum(uf, axis=1)
    count = jnp.arange(1, s + 1, dtype=jnp.float32)[None, :, None]
    outs = []
    for g, win in enumerate(POOL_WINDOWS):
        sl = slice(g * POOL_GROUP_DIM, (g + 1) * POOL_GROUP_DIM)
        c = cs[..., sl]
        lag = jnp.pad(c, ((0, 0), (win, 0), (0, 0)))[:, :s]
        outs.append((c - lag) / jnp.minimum(count, float(win)) - uf[..., sl])
    p = jnp.stack(outs, axis=2).astype(u.dtype)
    y = jnp.einsum("bsgc,gcd->bsgd", p, pool_w).reshape(bsz, s, POOL_WIDTH)
    return y * pool_scale

def rg_lru(u, conv_w, conv_b, w_r, b_r, w_i, b_i, lam):
    v = causal_depthwise_conv(u, conv_w) + conv_b
    bsz, s, _ = v.shape
    vh = v.reshape(bsz, s, LRU_HEADS, LRU_HEAD_DIM)
    r = jax.nn.sigmoid(jnp.einsum("bshc,hcd->bshd", vh, w_r).reshape(bsz, s, LRU_WIDTH) + b_r)
    i = jax.nn.sigmoid(jnp.einsum("bshc,hcd->bshd", vh, w_i).reshape(bsz, s, LRU_WIDTH) + b_i)
    log_a = -LRU_C * r.astype(jnp.float32) * jax.nn.softplus(-lam.astype(jnp.float32))
    a = jnp.exp(log_a)
    bterm = jnp.sqrt(-jnp.expm1(2.0 * log_a)) * (i * v).astype(jnp.float32)

    def combine(left, right):
        a1, b1 = left
        a2, b2 = right
        return a1 * a2, a2 * b1 + b2

    _, h = lax.associative_scan(combine, (a, bterm), axis=1)
    return h.astype(u.dtype)

def gated_short_conv(b_gate, c_gate, h, conv_w, w_out):
    return (b_gate * causal_depthwise_conv(c_gate * h, conv_w)) @ w_out

def hybrid_mixer(x, w_in, b_in, pool_w, pool_scale, lru_conv_w, lru_conv_b,
                 lru_w_r, lru_b_r, lru_w_i, lru_b_i, lru_lambda, lru_w_out,
                 sconv_w, sconv_w_out, w_mix_out):
    bsz, s, _ = x.shape
    z = x @ w_in + b_in
    z_pool, z_lru, z_b, z_c, z_h, z_gate = jnp.split(z, SPLIT_POINTS, axis=-1)
    y_pool = multiscale_pool(z_pool, pool_w, pool_scale)
    y_lru = rg_lru(z_lru, lru_conv_w, lru_conv_b, lru_w_r, lru_b_r,
                   lru_w_i, lru_b_i, lru_lambda) @ lru_w_out
    y_conv = gated_short_conv(z_b, z_c, z_h, sconv_w, sconv_w_out)
    gates = jax.nn.sigmoid(z_gate).reshape(bsz, s, N_BRANCH, D_MODEL)
    merged = (gates[:, :, 0] * y_pool + gates[:, :, 1] * y_lru
              + gates[:, :, 2] * y_conv)
    return merged @ w_mix_out

def memory_cross_attention(x, mem, w_q, w_k, w_v, w_o):
    bsz, s, _ = x.shape
    m = mem.shape[1]
    q = (x @ w_q).reshape(bsz, s, X_HEADS, X_HEAD_DIM)
    k = (mem @ w_k).reshape(bsz, m, X_HEADS, X_HEAD_DIM)
    v = (mem @ w_v).reshape(bsz, m, X_HEADS, X_HEAD_DIM)
    scores = jnp.einsum("bshd,bmhd->bhsm", q, k).astype(jnp.float32) * (X_HEAD_DIM ** -0.5)
    p = jax.nn.softmax(scores, axis=-1).astype(x.dtype)
    o = jnp.einsum("bhsm,bmhd->bshd", p, v).reshape(bsz, s, D_MODEL)
    return o @ w_o

def swiglu(x, w_gate, w_up, w_down):
    return (jax.nn.silu(x @ w_gate) * (x @ w_up)) @ w_down

def setup_inputs(seed: int = 0) -> dict:
    key = jax.random.key(seed)
    ks = jax.random.split(key, 28)

    def nrm(k, shape, scale):
        return jax.random.normal(k, shape, jnp.float32) * scale

    a0 = jax.random.uniform(ks[12], (DEPTH, LRU_WIDTH), jnp.float32, 0.9, 0.999)
    sig = a0 ** (1.0 / LRU_C)
    lru_lambda = jnp.log(sig) - jnp.log1p(-sig)
    return {
        "x": nrm(ks[0], (BATCH, SEQ, D_MODEL), 1.0),
        "mem": nrm(ks[1], (BATCH, N_MEM, D_MODEL), 1.0),
        "w_in": nrm(ks[2], (DEPTH, D_MODEL, IN_COLS), D_MODEL ** -0.5),
        "b_in": nrm(ks[3], (DEPTH, IN_COLS), 0.02),
        "pool_w": nrm(ks[4], (DEPTH, POOL_GROUPS, POOL_GROUP_DIM, POOL_GROUP_DIM), POOL_GROUP_DIM ** -0.5),
        "pool_scale": 1.0 + nrm(ks[5], (DEPTH, POOL_WIDTH), 0.1),
        "lru_conv_w": nrm(ks[6], (DEPTH, LRU_CONV, LRU_WIDTH), LRU_CONV ** -0.5),
        "lru_conv_b": nrm(ks[7], (DEPTH, LRU_WIDTH), 0.02),
        "lru_w_r": nrm(ks[8], (DEPTH, LRU_HEADS, LRU_HEAD_DIM, LRU_HEAD_DIM), LRU_HEAD_DIM ** -0.5),
        "lru_b_r": nrm(ks[9], (DEPTH, LRU_WIDTH), 0.02),
        "lru_w_i": nrm(ks[10], (DEPTH, LRU_HEADS, LRU_HEAD_DIM, LRU_HEAD_DIM), LRU_HEAD_DIM ** -0.5),
        "lru_b_i": nrm(ks[11], (DEPTH, LRU_WIDTH), 0.02),
        "lru_lambda": lru_lambda,
        "lru_w_out": nrm(ks[13], (DEPTH, LRU_WIDTH, D_MODEL), LRU_WIDTH ** -0.5),
        "sconv_w": nrm(ks[14], (DEPTH, SCONV_K, SCONV_WIDTH), SCONV_K ** -0.5),
        "sconv_w_out": nrm(ks[15], (DEPTH, SCONV_WIDTH, D_MODEL), SCONV_WIDTH ** -0.5),
        "w_mix_out": nrm(ks[16], (DEPTH, D_MODEL, D_MODEL), BETA * D_MODEL ** -0.5),
        "xa_w_q": nrm(ks[17], (DEPTH, D_MODEL, D_MODEL), D_MODEL ** -0.5),
        "xa_w_k": nrm(ks[18], (DEPTH, D_MODEL, D_MODEL), D_MODEL ** -0.5),
        "xa_w_v": nrm(ks[19], (DEPTH, D_MODEL, D_MODEL), BETA * D_MODEL ** -0.5),
        "xa_w_o": nrm(ks[20], (DEPTH, D_MODEL, D_MODEL), BETA * D_MODEL ** -0.5),
        "ffn_w_gate": nrm(ks[21], (DEPTH, D_MODEL, D_FF), D_MODEL ** -0.5),
        "ffn_w_up": nrm(ks[22], (DEPTH, D_MODEL, D_FF), D_MODEL ** -0.5),
        "ffn_w_down": nrm(ks[23], (DEPTH, D_FF, D_MODEL), BETA * D_FF ** -0.5),
        "ln_g": 1.0 + nrm(ks[24], (DEPTH, 3, D_MODEL), 0.05),
        "ln_b": nrm(ks[25], (DEPTH, 3, D_MODEL), 0.02),
    }

def reference(x, mem, w_in, b_in, pool_w, pool_scale, lru_conv_w, lru_conv_b,
              lru_w_r, lru_b_r, lru_w_i, lru_b_i, lru_lambda, lru_w_out,
              sconv_w, sconv_w_out, w_mix_out, xa_w_q, xa_w_k, xa_w_v, xa_w_o,
              ffn_w_gate, ffn_w_up, ffn_w_down, ln_g, ln_b):
    for l in range(DEPTH):
        mix = hybrid_mixer(x, w_in[l], b_in[l], pool_w[l], pool_scale[l],
                           lru_conv_w[l], lru_conv_b[l], lru_w_r[l], lru_b_r[l],
                           lru_w_i[l], lru_b_i[l], lru_lambda[l], lru_w_out[l],
                           sconv_w[l], sconv_w_out[l], w_mix_out[l])
        x = layer_norm(ALPHA * x + mix, ln_g[l, 0], ln_b[l, 0])
        xa = memory_cross_attention(x, mem, xa_w_q[l], xa_w_k[l], xa_w_v[l], xa_w_o[l])
        x = layer_norm(ALPHA * x + xa, ln_g[l, 1], ln_b[l, 1])
        ff = swiglu(x, ffn_w_gate[l], ffn_w_up[l], ffn_w_down[l])
        x = layer_norm(ALPHA * x + ff, ln_g[l, 2], ln_b[l, 2])
    return x


_drawn_inputs = setup_inputs


def setup_inputs(seed=0):
    import zlib

    import numpy as np

    out = dict(_drawn_inputs(seed))
    spreads = {}
    factors = {'lru_b_r': 64.0, 'lru_b_i': 50.336}
    for name, (base, spread) in spreads.items():
        noise = np.random.default_rng([zlib.crc32(name.encode()), seed]).standard_normal(out[name].shape)
        drawn = base * np.exp(spread * noise) if base else spread * noise
        out[name] = __import__('jax').numpy.asarray(drawn.astype(out[name].dtype))
    for name, factor in factors.items():
        out[name] = (out[name] * factor).astype(out[name].dtype)
    return out
```

```python
from contextlib import ExitStack

import concourse.bass as bass
from concourse import mybir

ALU = mybir.AluOpType
ACT = mybir.ActivationFunctionType
AX = mybir.AxisListType
F32 = mybir.dt.float32
F32R = mybir.dt.float32r

P = 128
SPLIT_SLOTS = 4
RAW_SLOTS = 2
LOOKAHEAD = SPLIT_SLOTS - 1
LN_EPS = 1e-5
POOL_WINDOWS = (2, 4, 8, 16)
POOL_PAD = max(POOL_WINDOWS)
LRU_TAPS = 4
SCONV_TAPS = 3
TINY = 2.0 ** -100

(B_POOL, B_LRU, B_B, B_C, B_H, B_GATE0, B_GATE1, B_GATE2, POOL_SCALE, LRU_W0, LRU_W1, LRU_W2, LRU_W3,
 LRU_B, RATE_R_B, RATE_I_B, LAMBDA, SC_W0, SC_W1, SC_W2, DECAY) = range(21)


class Signal:

    def __init__(self, sem, credit=0):
        self.sem, self.credit = sem, credit

    def done(self, n):
        return n + (1 + self.credit)


def hybrid_layer(nc, x, mem, w_in, b_in, pool_w, pool_scale, lru_conv_w, lru_conv_b, lru_w_r, lru_b_r,
                 lru_w_i, lru_b_i, lru_lambda, lru_w_out, sconv_w, sconv_w_out, w_mix_out, xa_w_q,
                 xa_w_k, xa_w_v, xa_w_o, ffn_w_gate, ffn_w_up, ffn_w_down, ln_g, ln_b, out):
    _, SEQ, D = x.shape
    M = mem.shape[1]
    FF = ffn_w_gate.shape[2]
    DEPTH = w_in.shape[0]
    ALPHA = (2 * DEPTH) ** 0.25
    KT = D // P
    TT = SEQ // P
    MT = M // P
    HT = FF // P
    HEADS = 4
    HD = D // HEADS
    SCORE_SCALE = float(HD) ** -0.5
    GROUPS = len(POOL_WINDOWS)
    COLS = 2048 // KT
    HALF = D // 2
    assert DEPTH == 1 and SEQ == 512 and COLS == 256 and HD == 256 and D == 1024

    A_BODY, B_BODY, F_BODY, G_BODY = 12, 20, 4, 4
    A_ITERS, B_ITERS, F_ITERS = GROUPS, KT // 4, HT // 2
    HEAD_STEPS = 6
    A0 = 0
    B0 = A0 + A_BODY * A_ITERS
    C0 = B0 + B_BODY * B_ITERS
    D0 = C0 + KT
    E0 = D0 + HEAD_STEPS * HEADS
    F0 = E0 + KT
    G0 = F0 + F_BODY * F_ITERS
    G_ITERS = (HT - 6) // G_BODY
    G_TAIL = HT - G_ITERS * G_BODY
    STEPS = G0 + HT
    S_UNIT = 3

    with ExitStack() as ctx:
        def sb(name, shape, dt=F32, where=ctx):
            return where.enter_context(nc.sbuf_tensor(name, shape, dt))

        def signal(name, credit=0):
            return Signal(ctx.enter_context(nc.semaphore(name)), credit)

        ident = sb("ident", [P, P])
        par = sb("par", [P, DECAY + 1, KT])
        corr = sb("corr", [P, GROUPS, POOL_PAD])
        inv_win = sb("inv_win", [P, GROUPS])
        xT_h = sb("xT_h", [P, KT, SEQ], F32R)
        xT_l = sb("xT_l", [P, KT, SEQ], F32R)
        raw = sb("raw", [P, RAW_SLOTS, 2048])
        wh = sb("wh", [P, SPLIT_SLOTS, 1024], F32R)
        wl = sb("wl", [P, SPLIT_SLOTS, 1024], F32R)
        act32 = sb("act32", [P, KT, SEQ])

        cur = sb("cur", [P, DECAY + 1, 2])
        cur_b = sb("cur_b", [P, 3, 4])
        soft = sb("soft", [P, 8, KT])
        stats = sb("stats", [P, TT, 2, 6])
        mean_var = sb("mean_var", [P, TT, 2])
        var_eps = sb("var_eps", [P, TT])
        dev = sb("dev", [P, TT])
        rstd = sb("rstd", [P, TT])
        row_max = sb("row_max", [P, TT])
        neg_max = sb("neg_max", [P, TT])
        row_sum = sb("row_sum", [P, TT])
        inv_sum = sb("inv_sum", [P, TT])

        with ExitStack() as scope:
            lru_h = sb("lru_h", [P, KT, SEQ], F32R, scope)
            lru_l = sb("lru_l", [P, KT, SEQ], F32R, scope)
            cnv_h = sb("cnv_h", [P, KT, SEQ], F32R, scope)
            cnv_l = sb("cnv_l", [P, KT, SEQ], F32R, scope)
        xnat = sb("xnat", [P, TT, D])
        gb = sb("gb", [P, 2, D])
        st_h = sb("st_h", [P, SPLIT_SLOTS, SEQ], F32R)
        st_l = sb("st_l", [P, SPLIT_SLOTS, SEQ], F32R)
        kT_h = sb("kT_h", [P, 2, M], F32R)
        kT_l = sb("kT_l", [P, 2, M], F32R)
        v_h = sb("v_h", [P, 2, MT, HD], F32R)
        v_l = sb("v_l", [P, 2, MT, HD], F32R)
        qT_h = sb("qT_h", [P, 2, SEQ], F32R)
        qT_l = sb("qT_l", [P, 2, SEQ], F32R)
        probs = sb("probs", [P, TT, M])
        silu = probs[:].rearrange("p t m -> p (t m)").rearrange("p (l s) -> p l s", l=2)

        with ExitStack() as scope:
            u = sb("u", [P, POOL_PAD + SEQ], F32, scope)
            ws = sb("ws", [P, SEQ], F32, scope)
            p_h = sb("p_h", [P, 2, SEQ], F32R, scope)
            p_l = sb("p_l", [P, 2, SEQ], F32R, scope)
            zl = sb("zl", [P, LRU_TAPS - 1 + SEQ], F32, scope)
            v = sb("v", [P, 2, SEQ], F32, scope)
            vr_h = sb("vr_h", [P, 2, SEQ], F32R, scope)
            vr_l = sb("vr_l", [P, 2, SEQ], F32R, scope)
            c = sb("c", [P, 2, SEQ], F32, scope)
            ch = sb("ch", [P, SCONV_TAPS - 1 + SEQ], F32, scope)
            o = sb("o", [P, 2, SEQ], F32, scope)
            rt = sb("rt", [P, SEQ], F32, scope)
            u1 = sb("u1", [P, SEQ], F32, scope)
            sq = sb("sq", [P, SEQ], F32, scope)
            ig = sb("ig", [P, SEQ], F32, scope)
        with ExitStack() as scope:
            gates = sb("gates", [P, 3, 2, SEQ], F32, scope)
            memT_h = sb("memT_h", [P, KT, M], F32R, scope)
            memT_l = sb("memT_l", [P, KT, M], F32R, scope)
            mem_nat = sb("mem_nat", [P, MT, D], F32, scope)
            pT_h = sb("pT_h", [P, MT, SEQ], F32R, scope)
            pT_l = sb("pT_l", [P, MT, SEQ], F32R, scope)
        with ExitStack() as scope:
            rows = sb("rows", [P, 2, P], F32, scope)
            tok1 = sb("tok1", [P, POOL_PAD], F32, scope)
        hidden = sb("hidden", [P, HT, SEQ])

        ps = ctx.enter_context(nc.psum_tensor("ps", [P, 8, 512], F32))

        x_in = [ctx.enter_context(nc.semaphore(f"x_in{t}")) for t in range(TT)]
        rows_in = ctx.enter_context(nc.semaphore("rows_in"))
        raw_in = [ctx.enter_context(nc.semaphore(f"raw_in{n}")) for n in range(RAW_SLOTS)]
        small_in = ctx.enter_context(nc.semaphore("small_in"))
        mem_in = ctx.enter_context(nc.semaphore("mem_in"))
        res_in = ctx.enter_context(nc.semaphore("res_in"))
        gb_in = ctx.enter_context(nc.semaphore("gb_in"))
        stored = ctx.enter_context(nc.semaphore("stored"))
        consts = signal("consts")
        ident_set = signal("ident_set")
        iv_done = signal("iv_done", 2)
        weights_used = signal("weights_used", SPLIT_SLOTS)
        par_full = signal("par_full")
        xt_full = signal("xt_full")
        tok_full = signal("tok_full")
        scores_full = signal("scores_full")
        pT_full = signal("pT_full")
        pv_full = signal("pv_full")
        w_hi = signal("w_hi")
        xt_hi = signal("xt_hi")
        soft_exp = signal("soft_exp")
        zl_full = signal("zl_full")
        v_tap0 = signal("v_tap0")
        vr_hi = signal("vr_hi")
        u_full = signal("u_full")
        p_hi = signal("p_hi", 1)
        c_full = signal("c_full")
        r_full = signal("r_full")
        i_full = signal("i_full", 2)
        t_full = signal("t_full")
        u1_full = signal("u1_full")
        sq_full = signal("sq_full")
        o_tap0 = signal("o_tap0")
        gate_full = signal("gate_full", 3)
        st_hi = signal("st_hi")
        dev_full = signal("dev_full")
        kT_hi = signal("kT_hi")
        v_hi = signal("v_hi")
        q_hi = signal("q_hi")
        exp_done = signal("exp_done")
        pT_hi = signal("pT_hi")
        silu_full = signal("silu_full", 1)
        w_lo = signal("w_lo", SPLIT_SLOTS)
        xt_lo = signal("xt_lo")
        par_done = signal("par_done")
        pads = signal("pads")
        corr_step = signal("corr_step")
        soft_step = signal("soft_step")
        cur_set = signal("cur_set")
        cur_b_set = signal("cur_b_set")
        conv_step = signal("conv_step", 1)
        pool_step = signal("pool_step", 1)
        vr_lo = signal("vr_lo")
        p_lo = signal("p_lo", 1)
        ypool = signal("ypool")
        lru_step = signal("lru_step", 1)
        sconv_step = signal("sconv_step", 6)
        out_step = signal("out_step", 4)
        merge_step = signal("merge_step", 7)
        st_lo = signal("st_lo")
        res_done = signal("res_done")
        ln_step = signal("ln_step")
        kT_lo = signal("kT_lo")
        v_lo = signal("v_lo")
        q_lo = signal("q_lo")
        max_step = signal("max_step")
        norm_step = signal("norm_step")
        pT_lo = signal("pT_lo")
        ot_full = signal("ot_full")
        h_full = signal("h_full", 1)

        CONV, POOL, LRU, SCONV, OUT, LN = 3, 3, 9, 3, 3, 7

        def merge_at(pair, step, l):
            return pair * 10 + 2 * step + l

        def cols(w, first):
            return w[0].rearrange("(k p) n -> p k n", p=P)[:, :, bass.ds(first, COLS)]

        def k_rows(w, first):
            return w[0].rearrange("(k p) n -> p k n", p=P)[:, bass.ds(first, 2), :]

        LOADS = {"A": (0, 0, 3, 2), "B": (12, 8, 5, 5), "C": (22, 18, 0, 0), "D": (24, 20, 0, 0),
                 "E": (30, 26, 0, 0), "F": (32, 28, 1, 1), "G": (43, 39, 1, 1)}
        FIRST = {"A": A0, "B": B0, "C": C0, "D": D0, "E": E0, "F": F0, "G": G0}
        BODY = {"A": A_BODY, "B": B_BODY, "C": 0, "D": 0, "E": 0, "F": F_BODY, "G": G_BODY}

        def wait_raw(eng, phase, it, unit):
            per_body = BODY[phase] // 2
            if per_body and unit >= per_body:
                it, unit = it + 1, unit - per_body
            n = unit // 2 if not (phase == "A" and unit > S_UNIT) else (unit - unit % 2) // 2 - unit % 2
            before, each = LOADS[phase][unit % 2], LOADS[phase][2 + unit % 2]
            eng.wait_ge(raw_in[unit % 2], 16 * (it * each + (before + n + 1)))

        def step_no(phase, it, s):
            return it * BODY[phase] + (FIRST[phase] + s)

        def is_small(phase, s):
            return phase == "A" and s % A_BODY // 2 == S_UNIT

        def raw_part(phase, s):
            r, half = s // 2 % RAW_SLOTS, s % 2
            size = 512 if is_small(phase, s) else 1024
            return raw[:, r, half * size:(half + 1) * size], size

        block = ctx.enter_context(nc.Block())

        @block.sync
        def _(sp):
            def load(phase, it, unit, *copies, sem=None):
                sp.wait_ge(w_lo.sem, w_lo.done(step_no(phase, it, 2 * unit - 3)))
                for dst, src in copies:
                    sp.dma_start(dst, src).then_inc(sem or raw_in[unit % 2], 16)

            def slot(unit):
                return raw[:, unit % RAW_SLOTS, :]

            def col_slot(unit):
                return slot(unit).rearrange("p (k n) -> p k n", k=KT)

            def row_slot(unit):
                return slot(unit).rearrange("p (k n) -> p k n", k=2)

            with sp.Fori(0, A_ITERS) as i:
                c0 = i * COLS
                load("A", i, 0, (col_slot(0), cols(w_in, c0 + D)))
                load("A", i, 1, (col_slot(1), cols(w_in, i * 2 * P)))
                load("A", i, 2, (col_slot(2), cols(w_in, c0 + 3 * D)))
                small = slot(3)
                load("A", i, S_UNIT,
                     (small[:, 0:512].rearrange("p (k n) -> p k n", k=2),
                      pool_w[0].rearrange("g (k p) n -> p (g k) n", p=P)[:, bass.ds(i * 2, 2), :]),
                     (small[:, 512:768].rearrange("p (h n) -> p h n", h=2),
                      lru_w_r[0].rearrange("h p n -> p h n")[:, bass.ds(i * 2, 2), :]),
                     (small[:, 768:1024].rearrange("p (h n) -> p h n", h=2),
                      lru_w_i[0].rearrange("h p n -> p h n")[:, bass.ds(i * 2, 2), :]),
                     sem=small_in)
                load("A", i, 4, (col_slot(4), cols(w_in, c0 + 4 * D)))
                load("A", i, 5, (col_slot(5), cols(w_in, c0 + 2 * D)))
            with sp.Fori(0, B_ITERS) as i:
                for q in range(2):
                    c0 = i * (2 * COLS) + q * COLS
                    for m in range(3):
                        load("B", i, 5 * q + m, (col_slot(5 * q + m), cols(w_in, c0 + (5 + m) * D)))
                    load("B", i, 5 * q + 3, (col_slot(5 * q + 3), cols(lru_w_out, i * 4 * P + q * COLS)))
                    load("B", i, 5 * q + 4, (col_slot(5 * q + 4), cols(sconv_w_out, i * 4 * P + q * COLS)))
            for n in range(KT // 2):
                load("C", 0, n, (row_slot(n), k_rows(w_mix_out, 2 * n)))
            for h in range(HEADS):
                for n, w in enumerate((xa_w_k, xa_w_v, xa_w_q)):
                    load("D", 0, 3 * h + n, (col_slot(3 * h + n), cols(w, h * HD)))
            for n in range(KT // 2):
                load("E", 0, n, (row_slot(n), k_rows(xa_w_o, 2 * n)))
            with sp.Fori(0, F_ITERS) as i:
                load("F", i, 0, (col_slot(0), cols(ffn_w_gate, i * COLS)))
                load("F", i, 1, (col_slot(1), cols(ffn_w_up, i * 2 * P)))
            with sp.Fori(0, G_ITERS) as i:
                load("G", i, 0, (row_slot(0), k_rows(ffn_w_down, i * 4)))
                load("G", i, 1, (row_slot(1), k_rows(ffn_w_down, i * 4 + 2)))
            for n in range(2 * G_ITERS, HT // 2):
                load("G", 0, n, (row_slot(n), k_rows(ffn_w_down, 2 * n)))
            for t in range(TT):
                sp.wait_ge(ln_step.sem, ln_step.done(LN * (2 * TT + t) + 6))
                sp.dma_start(out[0, t * P:(t + 1) * P, :], xnat[:, t, :]).then_inc(stored, 16)
            sp.wait_ge(stored, 16 * TT)

        @block.gpsimd
        def _(pool):
            def tiles(w):
                return w.rearrange("o (t p) -> (o t) p", p=P)

            at = 0
            for w in (tiles(b_in), tiles(pool_scale), lru_conv_w[0].rearrange("k (t p) -> (k t) p", p=P),
                      tiles(lru_conv_b), tiles(lru_b_r), tiles(lru_b_i), tiles(lru_lambda),
                      sconv_w[0].rearrange("k (t p) -> (k t) p", p=P)):
                n = w.shape[0]
                pool.dma_start(rows[at % P:at % P + n, at // P, :], w).then_inc(rows_in, 16)
                at += n
            nc.gpsimd.memset(ident[:], 0.0).then_inc(ident_set.sem, 1)
            pool.wait_ge(ident_set.sem, ident_set.done(0))
            nc.gpsimd.affine_select(out=ident[:], in_=ident[:], compare_op=ALU.not_equal, fill=1.0, base=0,
                                    pattern=[[-1, P]], channel_multiplier=1).then_inc(consts.sem, 1)
            nc.gpsimd.iota(tok1[:], pattern=[[1, POOL_PAD]], base=1, channel_multiplier=0,
                           allow_small_or_imprecise_dtypes=True).then_inc(consts.sem, 1)
            pool.sem_inc(iv_done.sem, iv_done.credit)
            with pool.Fori(0, A_ITERS) as i:
                for l in range(2):
                    j = i * 2 + l
                    pool.wait_ge(conv_step.sem, conv_step.done(j * CONV + 2))
                    pool.wait_ge(i_full.sem, i_full.done(j))
                    nc.gpsimd.tensor_tensor(ig[:], ig[:], v[:, l, :], ALU.mult).then_inc(iv_done.sem, 1)
            pool.wait_ge(lru_step.sem, lru_step.done(LRU * KT - 1))
            pool.wait_ge(out_step.sem, out_step.done(OUT * KT - 1))
            pool.dma_start(mem_nat[:], mem[0].rearrange("(t p) d -> p t d", p=P)).then_inc(mem_in, 16)
            pool.wait_ge(weights_used.sem, weights_used.done(C0 - 1))
            pool.dma_start(xnat[:], x[0].rearrange("(t p) d -> p t d", p=P)).then_inc(res_in, 16)
            for n in range(3):
                if n:
                    pool.wait_ge(ln_step.sem, ln_step.done(LN * n * TT - 1))
                pool.dma_start(gb[:, 0, :], ln_g[0, n:n + 1, :].broadcast_to([P, D])).then_inc(gb_in, 16)
                pool.dma_start(gb[:, 1, :], ln_b[0, n:n + 1, :].broadcast_to([P, D])).then_inc(gb_in, 16)

        @block.tensor
        def _(pe):
            def mm3(dst, st, st_lo_part, mv_, mv_lo_part, start, stop):
                nc.tensor.matmul(dst, st, mv_, start=start, stop=False)
                nc.tensor.matmul(dst, st, mv_lo_part, start=False, stop=False)
                return nc.tensor.matmul(dst, st_lo_part, mv_, start=False, stop=stop)

            def weights_ready(phase, it, s):
                pe.wait_ge(w_lo.sem, w_lo.done(step_no(phase, it, s)))

            def col_unit(phase, it, unit, bank, mh, ml, width=SEQ):
                for half in range(2):
                    s = 2 * unit + half
                    weights_ready(phase, it, s)
                    h_, l_ = (w[:, s % SPLIT_SLOTS, :].rearrange("p (k n) -> p k n", k=4) for w in (wh, wl))
                    for l in range(2):
                        for k in range(4):
                            last = mm3(ps[:, bank + l, 0:width],
                                       h_[:, k, l * P:(l + 1) * P], l_[:, k, l * P:(l + 1) * P],
                                       mh[:, 4 * half + k, :], ml[:, 4 * half + k, :],
                                       half == 0 and k == 0, half == 1 and k == 3)
                    last.then_inc(weights_used.sem, 1)

            def turn(src, tile, bank, width=4):
                for half in range(2):
                    for n in range(width):
                        k = 4 * half + n
                        last = nc.tensor.transpose(ps[:, bank + half, n * P:(n + 1) * P],
                                                   src[:, tile, k * P:(k + 1) * P], ident[:])
                    last.then_inc(xt_full.sem, 1)

            pe.sem_inc(weights_used.sem, weights_used.credit)
            pe.wait_ge(consts.sem, consts.done(0))
            x_nat0 = act32[:].rearrange("p k s -> p (k s)").rearrange("p (t d) -> p t d", t=TT)
            for t in range(TT):
                pe.wait_ge(x_in[t], 16)
                turn(x_nat0, t, 2 * t)
            pe.wait_ge(rows_in, 8 * 16)
            pe.wait_ge(xt_lo.sem, xt_lo.done(2 * TT - 1))
            nc.tensor.transpose(ps[:, 7, 0:P], rows[:, 0, :], ident[:])
            nc.tensor.transpose(ps[:, 7, P:P + 32], rows[0:32, 1, :], ident[0:32, 0:32]).then_inc(par_full.sem, 1)

            with pe.Fori(0, A_ITERS) as i:
                j1 = i * 2 + 1
                pe.wait_ge(i_full.sem, i_full.done(i * 2 - 2))
                col_unit("A", i, 0, 0, xT_h, xT_l)
                pe.wait_ge(i_full.sem, i_full.done(i * 2 - 1))
                col_unit("A", i, 1, 2, xT_h, xT_l)
                pe.wait_ge(sconv_step.sem, sconv_step.done(i * (2 * SCONV) - SCONV))
                col_unit("A", i, 2, 4, xT_h, xT_l)
                weights_ready("A", i, 6)
                pe.wait_ge(p_lo.sem, p_lo.done(j1))
                pe.wait_ge(par_done.sem, par_done.done(0))
                pe.wait_ge(out_step.sem, out_step.done(i * (2 * OUT) - OUT))
                h_, l_ = (w[:, 2, 0:512].rearrange("p (k n) -> p k n", k=2) for w in (wh, wl))
                for l in range(2):
                    for k in range(2):
                        last = mm3(ps[:, 6 + l, :], h_[:, k, l * P:(l + 1) * P], l_[:, k, l * P:(l + 1) * P],
                                   p_h[:, k, :], p_l[:, k, :], k == 0, k == 1)
                last.then_inc(weights_used.sem, 1)
                weights_ready("A", i, 7)
                pe.wait_ge(vr_lo.sem, vr_lo.done(j1))
                pe.wait_ge(u_full.sem, u_full.done(j1))
                for l in range(2):
                    for g in range(2):
                        at = (2 * g + l) * P
                        last = mm3(ps[:, 2 * l + g, :], wh[:, 3, at:at + P], wl[:, 3, at:at + P],
                                   vr_h[:, l, :], vr_l[:, l, :], True, True)
                last.then_inc(weights_used.sem, 1)
                pe.wait_ge(c_full.sem, c_full.done(j1))
                col_unit("A", i, 4, 4, xT_h, xT_l)
                pe.wait_ge(ypool.sem, ypool.done(j1))
                col_unit("A", i, 5, 6, xT_h, xT_l)

            with pe.Fori(0, B_ITERS) as i:
                pe.wait_ge(i_full.sem, i_full.done(KT - 2))
                pe.wait_ge(merge_step.sem, merge_step.done(i * 20 + (merge_at(-1, 1, 1))))
                col_unit("B", i, 0, 0, xT_h, xT_l)
                pe.wait_ge(i_full.sem, i_full.done(KT - 1))
                pe.wait_ge(merge_step.sem, merge_step.done(i * 20 + (merge_at(-1, 3, 1))))
                col_unit("B", i, 1, 2, xT_h, xT_l)
                pe.wait_ge(sconv_step.sem, sconv_step.done(SCONV * (KT - 1)))
                pe.wait_ge(gate_full.sem, gate_full.done(i * 12 - 3))
                col_unit("B", i, 2, 4, xT_h, xT_l)
                pe.wait_ge(out_step.sem, out_step.done(OUT * KT - 1))
                pe.wait_ge(gate_full.sem, gate_full.done(i * 12 - 1))
                pe.wait_ge(lru_step.sem, lru_step.done(LRU * KT - 1))
                col_unit("B", i, 3, 6, lru_h, lru_l)
                pe.wait_ge(gate_full.sem, gate_full.done(i * 12 + 1))
                col_unit("B", i, 4, 0, cnv_h, cnv_l)
                pe.wait_ge(gate_full.sem, gate_full.done(i * 12 + 3))
                col_unit("B", i, 5, 2, xT_h, xT_l)
                pe.wait_ge(gate_full.sem, gate_full.done(i * 12 + 5))
                col_unit("B", i, 6, 4, xT_h, xT_l)
                pe.wait_ge(merge_step.sem, merge_step.done(i * 20 + merge_at(0, 1, 1)))
                col_unit("B", i, 7, 6, xT_h, xT_l)
                pe.wait_ge(merge_step.sem, merge_step.done(i * 20 + merge_at(0, 3, 1)))
                col_unit("B", i, 8, 0, lru_h, lru_l)
                pe.wait_ge(gate_full.sem, gate_full.done(i * 12 + 7))
                col_unit("B", i, 9, 2, cnv_h, cnv_l)

            pe.wait_ge(mem_in, 16)
            pe.wait_ge(gate_full.sem, gate_full.done(6 * (KT // 2) - 1))
            for t in range(MT):
                turn(mem_nat, t, 4 + 2 * t)

            def accumulate(slot, bank, t, start, stop):
                for half in range(2):
                    last = mm3(ps[:, bank + half, :],
                               st_h[:, slot, t * P:(t + 1) * P], st_l[:, slot, t * P:(t + 1) * P],
                               wh[:, slot, half * HALF:(half + 1) * HALF], wl[:, slot, half * HALF:(half + 1) * HALF],
                               start, stop)
                return last

            def k_ready(phase, it, s, stage):
                weights_ready(phase, it, s)
                pe.wait_ge(st_lo.sem, st_lo.done(stage))

            def k_outer(phase, it, s, stage, start):
                k_ready(phase, it, s, stage)
                for t in range(TT):
                    last = accumulate(s % SPLIT_SLOTS, 2 * t, t, start, False)
                last.then_inc(weights_used.sem, 1)

            def last_four(phase, s0, stage0, t, bank):
                for n in range(4):
                    if t == 0:
                        k_ready(phase, 0, s0 + n, stage0 + n)
                    last = accumulate((s0 + n) % SPLIT_SLOTS, bank, t, False, n == 3)
                    if t == TT - 1:
                        last.then_inc(weights_used.sem, 1)
                if t < TT - 1:
                    last.then_inc(tok_full.sem, 1)

            for k in range(4):
                k_ready("C", 0, k, k)
                for t in range(TT):
                    if k == 0 and t == 0:
                        pe.wait_ge(merge_step.sem, merge_step.done(merge_at(KT // 2 - 1, 1, 1)))
                    if k == 0 and t == 1:
                        pe.wait_ge(merge_step.sem, merge_step.done(merge_at(KT // 2 - 1, 3, 1)))
                    if k == 0 and t >= 2:
                        pe.wait_ge(xt_lo.sem, xt_lo.done(8 + 2 * (t - 2) + 1))
                    last = accumulate(k, 2 * t, t, k == 0, False)
                last.then_inc(weights_used.sem, 1)
            for t in range(TT):
                last_four("C", 4, 4, t, 2 * t)
                if t == 2:
                    pe.wait_ge(ln_step.sem, ln_step.done(6))
                    turn(xnat, 0, 0)

            def turn_probs(h):
                pe.wait_ge(norm_step.sem, norm_step.done(5 * h + 4))
                for m in range(MT):
                    for t in range(TT):
                        last = nc.tensor.transpose(ps[:, 6 + m, t * P:(t + 1) * P],
                                                   probs[:, t, m * P:(m + 1) * P], ident[:])
                    last.then_inc(pT_full.sem, 1)

            def weigh_values(h):
                pe.wait_ge(pT_lo.sem, pT_lo.done(MT * h + 1))
                for d in range(2):
                    for m in range(MT):
                        last = mm3(ps[:, d, :], v_h[:, h % 2, m, d * P:(d + 1) * P], v_l[:, h % 2, m, d * P:(d + 1) * P],
                                   pT_h[:, m, :], pT_l[:, m, :], m == 0, m == MT - 1)
                    last.then_inc(pv_full.sem, 1)

            for h in range(HEADS):
                if h == 0:
                    pe.wait_ge(xt_lo.sem, xt_lo.done(12 + 1))
                elif h > 1:
                    pe.wait_ge(ot_full.sem, ot_full.done(2 * (h - 2) + 1))
                else:
                    pe.wait_ge(kT_lo.sem, kT_lo.done(1))
                pe.wait_ge(xt_lo.sem, xt_lo.done(8 + 3))
                col_unit("D", 0, 3 * h, 0, memT_h, memT_l, M)
                if h == 0:
                    pe.wait_ge(res_done.sem, res_done.done(3))
                else:
                    pe.wait_ge(v_lo.sem, v_lo.done(MT * h - 1))
                for half in range(2):
                    s = 2 * (3 * h + 1) + half
                    weights_ready("D", 0, s)
                    h_, l_ = (w[:, s % SPLIT_SLOTS, :].rearrange("p (k n) -> p k n", k=4) for w in (wh, wl))
                    for m in range(MT):
                        for k in range(4):
                            kk = 4 * half + k
                            last = mm3(ps[:, 2 + m, 0:HD],
                                       memT_h[:, kk, m * P:(m + 1) * P], memT_l[:, kk, m * P:(m + 1) * P],
                                       h_[:, k, :], l_[:, k, :], kk == 0, kk == KT - 1)
                    last.then_inc(weights_used.sem, 1)
                if h == 0:
                    for t, bank in ((1, 4), (2, 6), (3, 4)):
                        pe.wait_ge(ln_step.sem, ln_step.done(LN * t + 6))
                        if t < 3:
                            pe.wait_ge(res_done.sem, res_done.done(2 * (t + 1) + 1))
                        else:
                            pe.wait_ge(xt_lo.sem, xt_lo.done(12 + 3))
                        turn(xnat, t, bank)
                    pe.wait_ge(xt_lo.sem, xt_lo.done(12 + 7))
                else:
                    turn_probs(h - 1)
                    pe.wait_ge(q_lo.sem, q_lo.done(2 * h - 1))
                col_unit("D", 0, 3 * h + 2, 4, xT_h, xT_l)
                if h:
                    pe.wait_ge(kT_lo.sem, kT_lo.done(2 * h + 1))
                    weigh_values(h - 1)
                pe.wait_ge(kT_lo.sem, kT_lo.done(2 * h + 1))
                pe.wait_ge(q_lo.sem, q_lo.done(2 * h + 1))
                for t in range(TT):
                    for d in range(2):
                        last = mm3(ps[:, 6 + t // 2, t % 2 * M:(t % 2 + 1) * M],
                                   qT_h[:, d, t * P:(t + 1) * P], qT_l[:, d, t * P:(t + 1) * P],
                                   kT_h[:, d, :], kT_l[:, d, :], d == 0, d == 1)
                    if t % 2:
                        last.then_inc(scores_full.sem, 1)

            def e_bank(t):
                return (2 * t + 2) % 8

            for k in range(4):
                k_ready("E", 0, k, KT + k)
                if k == 0:
                    pe.wait_ge(v_lo.sem, v_lo.done(MT * HEADS - 1))
                    pe.wait_ge(q_lo.sem, q_lo.done(2 * HEADS - 1))
                for t in range(2):
                    accumulate(k, e_bank(t), t, k == 0, False)
            turn_probs(HEADS - 1)
            pe.wait_ge(ot_full.sem, ot_full.done(2 * HEADS - 3))
            weigh_values(HEADS - 1)
            pe.wait_ge(pT_lo.sem, pT_lo.done(MT * HEADS - 1))
            pe.wait_ge(ot_full.sem, ot_full.done(2 * HEADS - 1))
            for k in range(4):
                for t in range(2, TT):
                    last = accumulate(k, e_bank(t), t, k == 0, False)
                last.then_inc(weights_used.sem, 1)
            for t in range(TT):
                last_four("E", 4, KT + 4, t, e_bank(t))
                if t == 2:
                    pe.wait_ge(ln_step.sem, ln_step.done(LN * TT + 6))
                    turn(xnat, 0, e_bank(0))
            for t, bank in ((1, e_bank(1)), (2, e_bank(2)), (3, e_bank(0))):
                pe.wait_ge(ln_step.sem, ln_step.done(LN * (TT + t) + 6))
                if t == 3:
                    pe.wait_ge(xt_lo.sem, xt_lo.done(20 + 1))
                turn(xnat, t, bank)

            pe.wait_ge(xt_lo.sem, xt_lo.done(20 + 7))
            with pe.Fori(0, F_ITERS) as i:
                pe.wait_ge(silu_full.sem, silu_full.done(i * 2 - 1))
                col_unit("F", i, 0, 0, xT_h, xT_l)
                pe.wait_ge(h_full.sem, h_full.done(i * 2 - 1))
                col_unit("F", i, 1, 2, xT_h, xT_l)

            pe.wait_ge(silu_full.sem, silu_full.done(HT - 1))
            for k in range(G_BODY):
                k_ready("G", 0, k, 2 * KT + k)
                for t in range(TT):
                    if k == 0 and t == 1:
                        pe.wait_ge(h_full.sem, h_full.done(HT - 1))
                    last = accumulate(k, 2 * t, t, k == 0, False)
                last.then_inc(weights_used.sem, 1)
            with pe.Fori(1, G_ITERS) as i:
                for k in range(G_BODY):
                    k_outer("G", i, k, i * G_BODY + (2 * KT + k), False)
            for k in range(G_ITERS * G_BODY, HT - 4):
                k_outer("G", 0, k, 2 * KT + k, False)
            for t in range(TT):
                last_four("G", HT - 4, 2 * KT + HT - 4, t, 2 * t)

        @block.scalar
        def _(act):
            def split(phase, it, s):
                s += LOOKAHEAD
                act.wait_ge(weights_used.sem, weights_used.done(step_no(phase, it, s - SPLIT_SLOTS)))
                if is_small(phase, s):
                    act.wait_ge(small_in, 48 * (it + 1))
                elif s % 2 == 0:
                    wait_raw(act, phase, it, s // 2)
                src, size = raw_part(phase, s)
                nc.scalar.activation(wh[:, s % SPLIT_SLOTS, 0:size], src, ACT.Copy).then_inc(w_hi.sem, 1)

            def turned(first, t, bank, dst, width):
                for half in range(2):
                    act.wait_ge(xt_full.sem, xt_full.done(first + half))
                    nc.scalar.activation(dst[:, 4 * half:4 * half + 4, t * P:(t + 1) * P],
                                         ps[:, bank + half, :].rearrange("p (k q) -> p k q", k=4),
                                         ACT.Copy).then_inc(xt_hi.sem, 1)

            def stage(source_ready, src, n, slot):
                source_ready()
                nc.scalar.activation(st_h[:, slot, :], src, ACT.Copy).then_inc(st_hi.sem, 1)

            def stage_c(k):
                stage(lambda: act.wait_ge(merge_step.sem, merge_step.done(merge_at(k // 2, 4, k % 2))),
                      act32[:, k, :], k, k % SPLIT_SLOTS)

            def stage_e(k):
                stage(lambda: act.wait_ge(ot_full.sem, ot_full.done(k)), act32[:, k, :], k, k % SPLIT_SLOTS)

            def deviation(n, t):
                act.wait_ge(ln_step.sem, ln_step.done(LN * (n * TT + t) + 3))
                nc.scalar.activation(dev[:, t:t + 1], var_eps[:, t:t + 1], ACT.Sqrt).then_inc(dev_full.sem, 1)

            for s in (p_hi, i_full, gate_full, silu_full):
                act.sem_inc(s.sem, s.credit)
            for t in range(TT):
                act.dma_start(act32[:].rearrange("p k s -> p (k s)")[:, t * D:(t + 1) * D],
                              x[0, t * P:(t + 1) * P, :]).then_inc(x_in[t], 16)
            split("A", 0, -3)
            split("A", 0, -2)
            for t in range(TT):
                turned(2 * t, t, 2 * t, xT_h, P)
            split("A", 0, -1)
            act.wait_ge(soft_step.sem, soft_step.done(1))
            nc.scalar.activation(soft[:, 2, :], soft[:, 1, :], ACT.Exp).then_inc(soft_exp.sem, 1)

            def gate_chain(i, l):
                j = i * 2 + l
                act.wait_ge(weights_used.sem, weights_used.done(step_no("A", i, 7)))
                act.wait_ge(lru_step.sem, lru_step.done(j * LRU - 1))
                nc.scalar.activation(rt[:], ps[:, 2 * l, :], ACT.Sigmoid,
                                     bias=cur[:, RATE_R_B, l:l + 1]).then_inc(r_full.sem, 1)
                nc.scalar.activation(ig[:], ps[:, 2 * l + 1, :], ACT.Sigmoid,
                                     bias=cur[:, RATE_I_B, l:l + 1]).then_inc(i_full.sem, 1)
                act.wait_ge(r_full.sem, r_full.done(j))
                nc.scalar.activation(rt[:], rt[:], ACT.Tanh, scale=cur[:, DECAY, l:l + 1]).then_inc(t_full.sem, 1)
                act.wait_ge(t_full.sem, t_full.done(j))
                nc.scalar.activation(u1[:], rt[:], ACT.Copy, bias=1.0).then_inc(u1_full.sem, 1)
                act.wait_ge(lru_step.sem, lru_step.done(j * LRU))
                nc.scalar.activation(sq[:], sq[:], ACT.Sqrt).then_inc(sq_full.sem, 1)

            with act.Fori(0, A_ITERS) as i:
                for s in range(A_BODY):
                    split("A", i, s)
                    if s in (2, 3):
                        l = s - 2
                        j = i * 2 + l
                        if l == 0:
                            act.wait_ge(cur_set.sem, cur_set.done(i))
                        act.wait_ge(weights_used.sem, weights_used.done(step_no("A", i, 1)))
                        act.wait_ge(conv_step.sem, conv_step.done(j * CONV - 1))
                        nc.scalar.activation(zl[:, LRU_TAPS - 1:], ps[:, l, :], ACT.Identity,
                                             bias=cur[:, B_LRU, l:l + 1]).then_inc(zl_full.sem, 1)
                        act.wait_ge(zl_full.sem, zl_full.done(j))
                        act.wait_ge(iv_done.sem, iv_done.done(j - 2))
                        nc.scalar.activation(v[:, l, :], zl[:, 0:SEQ], ACT.Identity,
                                             scale=cur[:, LRU_W0, l:l + 1],
                                             bias=cur[:, LRU_B, l:l + 1]).then_inc(v_tap0.sem, 1)
                    if s in (3, 4):
                        j = i * 2 + (s - 3)
                        act.wait_ge(conv_step.sem, conv_step.done(j * CONV + 2))
                        nc.scalar.activation(vr_h[:, s - 3, :], v[:, s - 3, :], ACT.Copy).then_inc(vr_hi.sem, 1)
                    if s in (4, 5):
                        l = s - 4
                        j = i * 2 + l
                        act.wait_ge(weights_used.sem, weights_used.done(step_no("A", i, 3)))
                        act.wait_ge(pool_step.sem, pool_step.done(j * POOL - 1))
                        nc.scalar.activation(u[:, POOL_PAD:], ps[:, 2 + l, :], ACT.Identity,
                                             bias=cur[:, B_POOL, l:l + 1]).then_inc(u_full.sem, 1)
                        act.wait_ge(pool_step.sem, pool_step.done(j * POOL + 2))
                        nc.scalar.activation(p_h[:, l, :], ws[:], ACT.Copy).then_inc(p_hi.sem, 1)
                    if s in (6, 7):
                        l = s - 6
                        j = i * 2 + l
                        act.wait_ge(weights_used.sem, weights_used.done(step_no("A", i, 5)))
                        act.wait_ge(sconv_step.sem, sconv_step.done(j * SCONV - 2 * SCONV))
                        nc.scalar.activation(c[:, l, :], ps[:, 4 + l, :], ACT.Identity,
                                             bias=cur[:, B_C, l:l + 1]).then_inc(c_full.sem, 1)
                    if s in (8, 10):
                        gate_chain(i, (s - 8) // 2)
                    if s in (10, 11):
                        l = s - 10
                        j = i * 2 + l
                        act.wait_ge(sconv_step.sem, sconv_step.done(j * SCONV))
                        act.wait_ge(out_step.sem, out_step.done(j * OUT - (2 * OUT - 2)))
                        nc.scalar.activation(o[:, l, :], ch[:, 0:SEQ], ACT.Identity,
                                             scale=cur[:, SC_W0, l:l + 1]).then_inc(o_tap0.sem, 1)

            with act.Fori(0, B_ITERS) as i:
                for s in range(B_BODY):
                    split("B", i, s)
                    q, at = s // 10, s % 10
                    if at in (2, 4, 6):
                        m = at // 2 - 1
                        if s == 2:
                            act.wait_ge(cur_b_set.sem, cur_b_set.done(i))
                        act.wait_ge(weights_used.sem, weights_used.done(step_no("B", i, s - 1)))
                        act.wait_ge(merge_step.sem, merge_step.done(i * 20 + merge_at(q - 1, 4, 1)))
                        for l in range(2):
                            nc.scalar.activation(gates[:, m, l, :], ps[:, (0, 2)[q] + 2 * m + l, :], ACT.Sigmoid,
                                                 bias=cur_b[:, m, 2 * q + l:2 * q + l + 1]).then_inc(gate_full.sem, 1)

            for k in range(LOOKAHEAD):
                if k == 0:
                    act.wait_ge(weights_used.sem, weights_used.done(C0 - 1))
                stage_c(k)
            for t in range(MT):
                turned(8 + 2 * t, t, 4 + 2 * t, memT_h, P)
            for s in range(5):
                split("C", 0, s)
                stage_c(s + LOOKAHEAD)
            for t in range(3):
                deviation(0, t)
            turned(12, 0, 0, xT_h, P)
            for s in (5, 6, 7):
                split("C", 0, s)
            split("D", 0, 0)
            deviation(0, 3)

            def exps(h):
                for t in range(TT):
                    act.wait_ge(max_step.sem, max_step.done(4 * h + 2 * (t // 2) + 1))
                    nc.scalar.activation(probs[:, t, :], ps[:, 6 + t // 2, t % 2 * M:(t % 2 + 1) * M], ACT.Exp,
                                         scale=SCORE_SCALE, bias=neg_max[:, t:t + 1],
                                         accum_out=row_sum[:, t:t + 1]).then_inc(exp_done.sem, 1)

            def probs_hi(h):
                for m in range(MT):
                    act.wait_ge(pT_full.sem, pT_full.done(MT * h + m))
                    nc.scalar.activation(pT_h[:, m, :], ps[:, 6 + m, :], ACT.Copy).then_inc(pT_hi.sem, 1)

            for h in range(HEADS):
                base = HEAD_STEPS * h
                for s in range(HEAD_STEPS):
                    if h or s:
                        split("D", 0, base + s)
                    if s == 2:
                        act.wait_ge(weights_used.sem, weights_used.done(D0 + base + 1))
                        for d in range(2):
                            nc.scalar.activation(kT_h[:, d, :], ps[:, d, 0:M], ACT.Copy).then_inc(kT_hi.sem, 1)
                    if s == 4:
                        act.wait_ge(weights_used.sem, weights_used.done(D0 + base + 3))
                        for m in range(MT):
                            nc.scalar.activation(v_h[:, h % 2, m, :], ps[:, 2 + m, 0:HD], ACT.Copy).then_inc(v_hi.sem, 1)
                        if h == 0:
                            for t, bank in ((1, 4), (2, 6), (3, 4)):
                                turned(12 + 2 * t, t, bank, xT_h, P)
                        else:
                            probs_hi(h - 1)
                if h == HEADS - 1:
                    for k in range(4):
                        stage_e(k)
                act.wait_ge(weights_used.sem, weights_used.done(D0 + base + 5))
                for d in range(2):
                    nc.scalar.activation(qT_h[:, d, :], ps[:, 4 + d, :], ACT.Copy).then_inc(q_hi.sem, 1)
                if h == HEADS - 1:
                    split("E", 0, 0)
                exps(h)
            probs_hi(HEADS - 1)

            for s in range(1, 5):
                split("E", 0, s)
                stage_e(s + LOOKAHEAD)
            for t in range(3):
                deviation(1, t)
            turned(20, 0, 2, xT_h, P)
            deviation(1, 3)
            for s in (5, 6, 7):
                split("E", 0, s)
            for t, bank in ((1, 4), (2, 6), (3, 2)):
                turned(20 + 2 * t, t, bank, xT_h, P)

            with act.Fori(0, F_ITERS) as i:
                for s in range(F_BODY):
                    split("F", i, s)
                    if s == 2:
                        act.wait_ge(weights_used.sem, weights_used.done(step_no("F", i, 1)))
                        act.wait_ge(h_full.sem, h_full.done(i * 2 - 1))
                        for l in range(2):
                            nc.scalar.activation(silu[:, l, :], ps[:, l, :], ACT.Silu).then_inc(silu_full.sem, 1)

            act.wait_ge(h_full.sem, h_full.done(HT - 1))
            for k in range(LOOKAHEAD):
                nc.scalar.activation(st_h[:, k, :], hidden[:, k, :], ACT.Copy).then_inc(st_hi.sem, 1)
            with act.Fori(0, G_ITERS) as i:
                for s in range(G_BODY):
                    split("G", i, s)
                    nc.scalar.activation(st_h[:, (s + LOOKAHEAD) % SPLIT_SLOTS, :],
                                         hidden[:, i * G_BODY + (s + LOOKAHEAD), :], ACT.Copy).then_inc(st_hi.sem, 1)
            for s in range(G_ITERS * G_BODY, HT - LOOKAHEAD):
                split("G", 0, s)
                nc.scalar.activation(st_h[:, (s + LOOKAHEAD) % SPLIT_SLOTS, :],
                                     hidden[:, s + LOOKAHEAD, :], ACT.Copy).then_inc(st_hi.sem, 1)
            for t in range(TT):
                deviation(2, t)

        @block.vector
        def _(dve):
            def split(phase, it, s):
                s += LOOKAHEAD
                dve.wait_ge(w_hi.sem, w_hi.done(step_no(phase, it, s)))
                src, size = raw_part(phase, s)
                slot = s % SPLIT_SLOTS
                nc.vector.tensor_tensor(wl[:, slot, 0:size], src, wh[:, slot, 0:size].bitcast(F32),
                                        ALU.subtract).then_inc(w_lo.sem, 1)

            def turned(first, t, bank, dst_h, dst):
                for half in range(2):
                    part = (slice(None), slice(4 * half, 4 * half + 4), slice(t * P, (t + 1) * P))
                    dve.wait_ge(xt_hi.sem, xt_hi.done(first + half))
                    nc.vector.tensor_tensor(dst[part], ps[:, bank + half, :].rearrange("p (k q) -> p k q", k=4),
                                            dst_h[part].bitcast(F32), ALU.subtract).then_inc(xt_lo.sem, 1)

            def stage(src, n, slot):
                dve.wait_ge(st_hi.sem, st_hi.done(n))
                nc.vector.tensor_tensor(st_l[:, slot, :], src, st_h[:, slot, :].bitcast(F32),
                                        ALU.subtract).then_inc(st_lo.sem, 1)

            def layer_norm(n, t, bank):
                first = LN * (n * TT + t)
                if t < TT - 1:
                    dve.wait_ge(tok_full.sem, tok_full.done(n * (TT - 1) + t))
                else:
                    dve.wait_ge(weights_used.sem, weights_used.done((C0, E0, G0)[n] + (KT, KT, HT)[n] - 1))
                if n == 0 and t == 0:
                    dve.wait_ge(res_in, 16)
                for half in range(2):
                    part = xnat[:, t, half * HALF:(half + 1) * HALF]
                    nc.vector.scalar_tensor_tensor(out=part, in0=part, scalar=ALPHA, in1=ps[:, bank + half, :],
                                                   op0=ALU.mult, op1=ALU.add).then_inc(res_done.sem, 1)
                for half in range(2):
                    dve.wait_ge(res_done.sem, res_done.done(2 * (n * TT + t) + half))
                    nc.vector.bn_stats(stats[:, t, half, :],
                                       xnat[:, t, half * HALF:(half + 1) * HALF]).then_inc(ln_step.sem, 1)
                dve.wait_ge(ln_step.sem, ln_step.done(first + 1))
                nc.vector.bn_aggr(mean_var[:, t, :], stats[:, t, :, :]).then_inc(ln_step.sem, 1)
                dve.wait_ge(ln_step.sem, ln_step.done(first + 2))
                nc.vector.tensor_scalar(var_eps[:, t:t + 1], mean_var[:, t, 1:2], LN_EPS, None,
                                        ALU.add).then_inc(ln_step.sem, 1)
                if t == 0:
                    dve.wait_ge(gb_in, 32 * (n + 1))
                row = xnat[:, t, :]
                nc.vector.scalar_tensor_tensor(out=row, in0=row, scalar=mean_var[:, t, 0:1], in1=gb[:, 0, :],
                                               op0=ALU.subtract, op1=ALU.mult).then_inc(ln_step.sem, 1)
                dve.wait_ge(dev_full.sem, dev_full.done(n * TT + t))
                nc.vector.reciprocal(rstd[:, t:t + 1], dev[:, t:t + 1]).then_inc(ln_step.sem, 1)
                dve.wait_ge(ln_step.sem, ln_step.done(first + 5))
                nc.vector.scalar_tensor_tensor(out=row, in0=row, scalar=rstd[:, t:t + 1], in1=gb[:, 1, :],
                                               op0=ALU.mult, op1=ALU.add).then_inc(ln_step.sem, 1)

            for s in (w_lo, conv_step, pool_step, p_lo, lru_step, sconv_step, out_step, merge_step, h_full):
                dve.sem_inc(s.sem, s.credit)
            for g, window in enumerate(POOL_WINDOWS):
                nc.vector.memset(inv_win[:, g:g + 1], 1.0 / window).then_inc(pads.sem, 1)
            dve.wait_ge(consts.sem, consts.done(1))
            nc.vector.reciprocal(tok1[:], tok1[:]).then_inc(corr_step.sem, 1)
            dve.wait_ge(corr_step.sem, corr_step.done(0))
            for g, window in enumerate(POOL_WINDOWS):
                nc.vector.tensor_scalar(corr[:, g, :], tok1[:], float(window), 1.0, ALU.mult,
                                        ALU.max).then_inc(corr_step.sem, 1)
            split("A", 0, -3)
            split("A", 0, -2)
            for t in range(TT):
                turned(2 * t, t, 2 * t, xT_h, xT_l)
            split("A", 0, -1)
            dve.wait_ge(par_full.sem, par_full.done(0))
            nc.vector.tensor_copy(par[:, 0:DECAY, :].rearrange("p r k -> p (r k)"),
                                  ps[:, 7, 0:DECAY * KT]).then_inc(par_done.sem, 1)
            dve.wait_ge(par_done.sem, par_done.done(0))

            n_soft = [0]

            def soft_op(ins):
                ins.then_inc(soft_step.sem, 1)
                dve.wait_ge(soft_step.sem, soft_step.done(n_soft[0]))
                n_soft[0] += 1

            neg, z, den, f, f2, acc = (soft[:, n, :] for n in (0, 2, 3, 5, 6, 7))
            soft_op(nc.vector.tensor_scalar(neg, par[:, LAMBDA, :], -1.0, None, ALU.mult))
            soft_op(nc.vector.tensor_tensor(soft[:, 1, :], neg, par[:, LAMBDA, :], ALU.min))
            dve.wait_ge(soft_exp.sem, soft_exp.done(0))
            soft_op(nc.vector.tensor_scalar(den, z, 2.0, None, ALU.add))
            soft_op(nc.vector.reciprocal(soft[:, 4, :], den))
            soft_op(nc.vector.tensor_tensor(f, z, soft[:, 4, :], ALU.mult))
            soft_op(nc.vector.tensor_tensor(f2, f, f, ALU.mult))
            soft_op(nc.vector.tensor_scalar(acc, f2, 1.0 / 17, None, ALU.mult))
            for n in range(7, 0, -1):
                soft_op(nc.vector.scalar_tensor_tensor(out=acc, in0=acc, scalar=1.0 / (2 * n + 1), in1=f2,
                                                       op0=ALU.add, op1=ALU.mult))
            soft_op(nc.vector.scalar_tensor_tensor(out=acc, in0=acc, scalar=1.0, in1=f, op0=ALU.add, op1=ALU.mult))
            soft_op(nc.vector.tensor_scalar(neg, neg, 0.0, 4.0, ALU.max, ALU.mult))
            soft_op(nc.vector.scalar_tensor_tensor(out=par[:, DECAY, :], in0=acc, scalar=8.0, in1=neg,
                                                   op0=ALU.mult, op1=ALU.add))
            nc.vector.memset(u[:, 0:POOL_PAD], 0.0).then_inc(pads.sem, 1)
            nc.vector.memset(zl[:, 0:LRU_TAPS - 1], 0.0).then_inc(pads.sem, 1)
            nc.vector.memset(ch[:, 0:SCONV_TAPS - 1], 0.0).then_inc(pads.sem, 1)
            dve.wait_ge(pads.sem, pads.done(2 + GROUPS))
            dve.wait_ge(corr_step.sem, corr_step.done(GROUPS))

            def conv_taps(i, l):
                j = i * 2 + l
                dve.wait_ge(v_tap0.sem, v_tap0.done(j))
                for k in range(1, LRU_TAPS):
                    if k > 1:
                        dve.wait_ge(conv_step.sem, conv_step.done(j * CONV + (k - 2)))
                    nc.vector.scalar_tensor_tensor(out=v[:, l, :], in0=zl[:, k:k + SEQ],
                                                   scalar=cur[:, LRU_W0 + k, l:l + 1], in1=v[:, l, :],
                                                   op0=ALU.mult, op1=ALU.add).then_inc(conv_step.sem, 1)

            def v_low(i, l):
                dve.wait_ge(vr_hi.sem, vr_hi.done(i * 2 + l))
                nc.vector.tensor_tensor(vr_l[:, l, :], v[:, l, :], vr_h[:, l, :].bitcast(F32),
                                        ALU.subtract).then_inc(vr_lo.sem, 1)

            def pool_tile(i, l):
                j = i * 2 + l
                dve.wait_ge(pads.sem, pads.done(2 + GROUPS))
                dve.wait_ge(u_full.sem, u_full.done(j))
                dve.wait_ge(p_hi.sem, p_hi.done(j - 1))
                dve.wait_ge(p_lo.sem, p_lo.done(j - 1))
                lag = u[:, bass.ds(lag_at, SEQ)]
                nc.vector.tensor_tensor_scan(ws[:], u[:, POOL_PAD:], lag, 0.0, ALU.add,
                                             ALU.subtract).then_inc(pool_step.sem, 1)
                dve.wait_ge(pool_step.sem, pool_step.done(j * POOL))
                nc.vector.tensor_tensor(ws[:, 0:POOL_PAD], ws[:, 0:POOL_PAD],
                                        corr[:, bass.ds(i, 1), :].rearrange("p g t -> p (g t)"),
                                        ALU.mult).then_inc(pool_step.sem, 1)
                dve.wait_ge(pool_step.sem, pool_step.done(j * POOL + 1))
                nc.vector.scalar_tensor_tensor(out=ws[:], in0=ws[:], scalar=inv_win[:, bass.ds(i, 1)],
                                               in1=u[:, POOL_PAD:], op0=ALU.mult,
                                               op1=ALU.subtract).then_inc(pool_step.sem, 1)
                dve.wait_ge(p_hi.sem, p_hi.done(j))
                nc.vector.tensor_tensor(p_l[:, l, :], ws[:], p_h[:, l, :].bitcast(F32),
                                        ALU.subtract).then_inc(p_lo.sem, 1)

            def lru_first(i, l):
                j = i * 2 + l
                dve.wait_ge(t_full.sem, t_full.done(j))
                nc.vector.tensor_scalar(sq[:], rt[:], TINY, None, ALU.max).then_inc(lru_step.sem, 1)
                dve.wait_ge(u1_full.sem, u1_full.done(j))
                nc.vector.reciprocal(u1[:], u1[:]).then_inc(lru_step.sem, 1)

            def lru_rest(i, l):
                j = i * 2 + l

                def after(n):
                    dve.wait_ge(lru_step.sem, lru_step.done(j * LRU + n))

                after(1)
                nc.vector.tensor_tensor(rt[:], rt[:], u1[:], ALU.mult).then_inc(lru_step.sem, 1)
                after(2)
                nc.vector.tensor_scalar(rt[:], rt[:], -2.0, 1.0, ALU.mult, ALU.add).then_inc(lru_step.sem, 1)
                dve.wait_ge(sq_full.sem, sq_full.done(j))
                nc.vector.scalar_tensor_tensor(out=sq[:], in0=u1[:], scalar=2.0, in1=sq[:], op0=ALU.mult,
                                               op1=ALU.mult).then_inc(lru_step.sem, 1)
                dve.wait_ge(iv_done.sem, iv_done.done(j))
                after(4)
                nc.vector.tensor_tensor(sq[:], sq[:], ig[:], ALU.mult).then_inc(lru_step.sem, 1)
                after(5)
                nc.vector.tensor_tensor_scan(u1[:], rt[:], sq[:], 0.0, ALU.mult, ALU.add).then_inc(lru_step.sem, 1)
                after(6)
                hi, lo = (b[:, bass.ds(j, 1), :].rearrange("p k s -> p (k s)") for b in (lru_h, lru_l))
                nc.vector.tensor_scalar(hi, u1[:], 1.0, None, ALU.mult).then_inc(lru_step.sem, 1)
                after(7)
                nc.vector.tensor_tensor(lo, u1[:], hi.bitcast(F32), ALU.subtract).then_inc(lru_step.sem, 1)

            def sconv(i, l):
                j = i * 2 + l
                dve.wait_ge(weights_used.sem, weights_used.done(step_no("A", i, 9)))
                dve.wait_ge(c_full.sem, c_full.done(j))
                dve.wait_ge(sconv_step.sem, sconv_step.done(j * SCONV - 1))
                nc.vector.scalar_tensor_tensor(out=ch[:, SCONV_TAPS - 1:], in0=ps[:, 4 + l, :],
                                               scalar=cur[:, B_H, l:l + 1], in1=c[:, l, :], op0=ALU.add,
                                               op1=ALU.mult).then_inc(sconv_step.sem, 1)
                dve.wait_ge(o_tap0.sem, o_tap0.done(j))
                for k in range(1, SCONV_TAPS):
                    if k > 1:
                        dve.wait_ge(sconv_step.sem, sconv_step.done(j * SCONV + (k - 1)))
                    nc.vector.scalar_tensor_tensor(out=o[:, l, :], in0=ch[:, k:k + SEQ],
                                                   scalar=cur[:, SC_W0 + k, l:l + 1], in1=o[:, l, :],
                                                   op0=ALU.mult, op1=ALU.add).then_inc(sconv_step.sem, 1)

            def conv_out(i, l):
                j = i * 2 + l
                if l == 0:
                    dve.wait_ge(weights_used.sem, weights_used.done(step_no("A", i, 11)))
                dve.wait_ge(sconv_step.sem, sconv_step.done(j * SCONV + 2))
                nc.vector.scalar_tensor_tensor(out=o[:, l, :], in0=ps[:, 6 + l, :], scalar=cur[:, B_B, l:l + 1],
                                               in1=o[:, l, :], op0=ALU.add, op1=ALU.mult).then_inc(out_step.sem, 1)
                hi, lo = (b[:, bass.ds(j, 1), :].rearrange("p k s -> p (k s)") for b in (cnv_h, cnv_l))
                dve.wait_ge(out_step.sem, out_step.done(j * OUT))
                nc.vector.tensor_scalar(hi, o[:, l, :], 1.0, None, ALU.mult).then_inc(out_step.sem, 1)
                dve.wait_ge(out_step.sem, out_step.done(j * OUT + 1))
                nc.vector.tensor_tensor(lo, o[:, l, :], hi.bitcast(F32), ALU.subtract).then_inc(out_step.sem, 1)

            with dve.Fori(0, A_ITERS) as i:
                lag_at = dve.snap(POOL_PAD - (POOL_WINDOWS[0] << i))
                nc.vector.tensor_scalar(cur[:], par[:, :, bass.ds(i * 2, 2)], 1.0, None,
                                        ALU.mult).then_inc(cur_set.sem, 1)
                dve.wait_ge(cur_set.sem, cur_set.done(i))
                for s in range(A_BODY):
                    split("A", i, s)
                    if s == 2:
                        conv_taps(i, 0)
                    if s == 3:
                        conv_taps(i, 1)
                        v_low(i, 0)
                    if s == 4:
                        pool_tile(i, 0)
                        v_low(i, 1)
                    if s == 5:
                        pool_tile(i, 1)
                    if s == 7:
                        for l in range(2):
                            if l == 0:
                                dve.wait_ge(weights_used.sem, weights_used.done(step_no("A", i, 6)))
                            nc.vector.tensor_scalar(
                                act32[:, bass.ds(i * 2 + l, 1), :].rearrange("p k s -> p (k s)"),
                                ps[:, 6 + l, :], cur[:, POOL_SCALE, l:l + 1], None, ALU.mult).then_inc(ypool.sem, 1)
                    if s == 8:
                        lru_first(i, 0)
                    if s == 9:
                        lru_rest(i, 0)
                    if s == 10:
                        lru_first(i, 1)
                        sconv(i, 0)
                    if s == 11:
                        sconv(i, 1)
                        lru_rest(i, 1)
                for l in range(2):
                    conv_out(i, l)

            with dve.Fori(0, B_ITERS) as i:
                nc.vector.tensor_scalar(cur_b[:], par[:, B_GATE0:B_GATE2 + 1, bass.ds(i * 4, 4)], 1.0, None,
                                        ALU.mult).then_inc(cur_b_set.sem, 1)

                def merge(q, step):
                    for l in range(2):
                        g0, g1, g2 = (gates[:, m, l, :] for m in range(3))
                        y = act32[:, bass.ds(i * 4 + (2 * q + l), 1), :].rearrange("p k s -> p (k s)")
                        before = merge_step.done(i * 20 + merge_at(q, step - 1, l))
                        if step == 0:
                            dve.wait_ge(gate_full.sem, gate_full.done(i * 12 + (6 * q + l)))
                            args = (g0, g0, y, ALU.mult)
                        elif step == 1:
                            dve.wait_ge(gate_full.sem, gate_full.done(i * 12 + (6 * q + 2 + l)))
                            dve.wait_ge(weights_used.sem, weights_used.done(step_no("B", i, 10 * q + 7)))
                            args = (g1, g1, ps[:, (6, 0)[q] + l, :], ALU.mult)
                        elif step == 2:
                            dve.wait_ge(merge_step.sem, before)
                            args = (g0, g0, g1, ALU.add)
                        elif step == 3:
                            dve.wait_ge(gate_full.sem, gate_full.done(i * 12 + (6 * q + 4 + l)))
                            dve.wait_ge(weights_used.sem, weights_used.done(step_no("B", i, 10 * q + 9)))
                            args = (g2, g2, ps[:, (0, 2)[q] + l, :], ALU.mult)
                        else:
                            dve.wait_ge(merge_step.sem, before)
                            args = (y, g0, g2, ALU.add)
                        nc.vector.tensor_tensor(*args).then_inc(merge_step.sem, 1)

                for s in range(B_BODY):
                    split("B", i, s)
                    q, at = s // 10, s % 10
                    if at == 2:
                        merge(q, 0)
                    if at == 8:
                        merge(q, 1)
                        merge(q, 2)
                    if s == 10:
                        merge(0, 3)
                        merge(0, 4)
                merge(1, 3)
                merge(1, 4)

            for k in range(LOOKAHEAD):
                stage(act32[:, k, :], k, k)
            for t in range(MT):
                turned(8 + 2 * t, t, 4 + 2 * t, memT_h, memT_l)
            for s in range(5):
                split("C", 0, s)
                k = s + LOOKAHEAD
                stage(act32[:, k, :], k, k % SPLIT_SLOTS)
            for t in range(3):
                layer_norm(0, t, 2 * t)
            turned(12, 0, 0, xT_h, xT_l)
            for s in (5, 6, 7):
                split("C", 0, s)
            split("D", 0, 0)
            layer_norm(0, 3, 6)

            def maxima(h):
                for b in range(2):
                    dve.wait_ge(scores_full.sem, scores_full.done(2 * h + b))
                    nc.vector.tensor_reduce(row_max[:, 2 * b:2 * b + 2],
                                            ps[:, 6 + b, :].rearrange("p (t m) -> p t m", t=2),
                                            AX.X, ALU.max).then_inc(max_step.sem, 1)
                    dve.wait_ge(max_step.sem, max_step.done(4 * h + 2 * b))
                    nc.vector.tensor_scalar(neg_max[:, 2 * b:2 * b + 2], row_max[:, 2 * b:2 * b + 2],
                                            -SCORE_SCALE, None, ALU.mult).then_inc(max_step.sem, 1)

            def normalise(h):
                dve.wait_ge(exp_done.sem, exp_done.done(TT * h + TT - 1))
                nc.vector.reciprocal(inv_sum[:], row_sum[:]).then_inc(norm_step.sem, 1)
                dve.wait_ge(norm_step.sem, norm_step.done(5 * h))
                for t in range(TT):
                    nc.vector.tensor_scalar(probs[:, t, :], probs[:, t, :], inv_sum[:, t:t + 1], None,
                                            ALU.mult).then_inc(norm_step.sem, 1)

            def probs_low(h):
                for m in range(MT):
                    dve.wait_ge(pT_hi.sem, pT_hi.done(MT * h + m))
                    nc.vector.tensor_tensor(pT_l[:, m, :], ps[:, 6 + m, :], pT_h[:, m, :].bitcast(F32),
                                            ALU.subtract).then_inc(pT_lo.sem, 1)

            def weighed(h):
                for d in range(2):
                    dve.wait_ge(pv_full.sem, pv_full.done(2 * h + d))
                    nc.vector.tensor_copy(act32[:, 2 * h + d, :], ps[:, d, :]).then_inc(ot_full.sem, 1)

            for h in range(HEADS):
                base = HEAD_STEPS * h
                for s in range(HEAD_STEPS):
                    if h or s:
                        split("D", 0, base + s)
                    if s == 2:
                        for d in range(2):
                            dve.wait_ge(kT_hi.sem, kT_hi.done(2 * h + d))
                            nc.vector.tensor_tensor(kT_l[:, d, :], ps[:, d, 0:M], kT_h[:, d, :].bitcast(F32),
                                                    ALU.subtract).then_inc(kT_lo.sem, 1)
                    if s == 4:
                        for m in range(MT):
                            dve.wait_ge(v_hi.sem, v_hi.done(MT * h + m))
                            nc.vector.tensor_tensor(v_l[:, h % 2, m, :], ps[:, 2 + m, 0:HD],
                                                    v_h[:, h % 2, m, :].bitcast(F32),
                                                    ALU.subtract).then_inc(v_lo.sem, 1)
                        if h == 0:
                            for t, bank in ((1, 4), (2, 6), (3, 4)):
                                turned(12 + 2 * t, t, bank, xT_h, xT_l)
                        else:
                            probs_low(h - 1)
                if h == HEADS - 1:
                    for k in range(4):
                        stage(act32[:, k, :], KT + k, k)
                for d in range(2):
                    dve.wait_ge(q_hi.sem, q_hi.done(2 * h + d))
                    nc.vector.tensor_tensor(qT_l[:, d, :], ps[:, 4 + d, :], qT_h[:, d, :].bitcast(F32),
                                            ALU.subtract).then_inc(q_lo.sem, 1)
                if h:
                    weighed(h - 1)
                if h == HEADS - 1:
                    split("E", 0, 0)
                maxima(h)
                normalise(h)
            probs_low(HEADS - 1)
            weighed(HEADS - 1)

            for s in range(1, 5):
                split("E", 0, s)
                k = s + LOOKAHEAD
                stage(act32[:, k, :], KT + k, k % SPLIT_SLOTS)
            for t in range(3):
                layer_norm(1, t, (2 * t + 2) % 8)
            turned(20, 0, 2, xT_h, xT_l)
            layer_norm(1, 3, 0)
            for s in (5, 6, 7):
                split("E", 0, s)
            for t, bank in ((1, 4), (2, 6), (3, 2)):
                turned(20 + 2 * t, t, bank, xT_h, xT_l)

            with dve.Fori(0, F_ITERS) as i:
                for s in range(F_BODY):
                    split("F", i, s)
                dve.wait_ge(weights_used.sem, weights_used.done(step_no("F", i, 3)))
                for l in range(2):
                    dve.wait_ge(silu_full.sem, silu_full.done(i * 2 + l))
                    nc.vector.tensor_tensor(hidden[:, bass.ds(i * 2 + l, 1), :].rearrange("p k s -> p (k s)"),
                                            silu[:, l, :], ps[:, 2 + l, :], ALU.mult).then_inc(h_full.sem, 1)

            for k in range(LOOKAHEAD):
                stage(hidden[:, k, :], 2 * KT + k, k)
            with dve.Fori(0, G_ITERS) as i:
                for s in range(G_BODY):
                    split("G", i, s)
                    k = s + LOOKAHEAD
                    stage(hidden[:, bass.ds(i * G_BODY + k, 1), :].rearrange("p k s -> p (k s)"),
                          i * G_BODY + (2 * KT + k), k % SPLIT_SLOTS)
            for s in range(G_ITERS * G_BODY, HT - LOOKAHEAD):
                split("G", 0, s)
                k = s + LOOKAHEAD
                stage(hidden[:, k, :], 2 * KT + k, k % SPLIT_SLOTS)
            for t in range(TT):
                layer_norm(2, t, 2 * t)


_INS = ["x", "mem", "w_in", "b_in", "pool_w", "pool_scale", "lru_conv_w", "lru_conv_b", "lru_w_r", "lru_b_r",
        "lru_w_i", "lru_b_i", "lru_lambda", "lru_w_out", "sconv_w", "sconv_w_out", "w_mix_out", "xa_w_q",
        "xa_w_k", "xa_w_v", "xa_w_o", "ffn_w_gate", "ffn_w_up", "ffn_w_down", "ln_g", "ln_b"]


def kernel(**inputs):
    import numpy as np
    import concourse.bacc as bacc
    from concourse.bass_utils import run_bass_kernel_spmd

    nc = bacc.Bacc("TRN2", target_bir_lowering=False, num_devices=1)
    arrays, args = {}, []
    for name in _INS:
        a = np.ascontiguousarray(inputs[name])
        arrays[f"in_{name}"] = a
        args.append(nc.dram_tensor(f"in_{name}", a.shape, mybir.dt.from_np(a.dtype), kind="ExternalInput").ap())
    out = nc.dram_tensor("out", arrays["in_x"].shape, F32, kind="ExternalOutput").ap()
    hybrid_layer(nc, *args, out)
    return run_bass_kernel_spmd(nc, [arrays], core_ids=[0]).results[0]["out"]
```

```python
from contextlib import ExitStack

import concourse.bass as bass
from concourse import mybir

ALU = mybir.AluOpType
ACT = mybir.ActivationFunctionType
AX = mybir.AxisListType
F32 = mybir.dt.float32
F32R = mybir.dt.float32r

P = 128
SPLIT_SLOTS = 4
RAW_SLOTS = 2
LOOKAHEAD = SPLIT_SLOTS - 1
LN_EPS = 1e-5
POOL_WINDOWS = (2, 4, 8, 16)
POOL_PAD = max(POOL_WINDOWS)
LRU_TAPS = 4
SCONV_TAPS = 3
TINY = 2.0 ** -100

(B_POOL, B_LRU, B_B, B_C, B_H, B_GATE0, B_GATE1, B_GATE2, POOL_SCALE, LRU_W0, LRU_W1, LRU_W2, LRU_W3,
 LRU_B, RATE_R_B, RATE_I_B, LAMBDA, SC_W0, SC_W1, SC_W2, DECAY, DECAY_EXP) = range(22)


class Signal:

    def __init__(self, sem, credit=0):
        self.sem, self.credit = sem, credit

    def done(self, n):
        return n + (1 + self.credit)


def hybrid_layer(nc, x, mem, w_in, b_in, pool_w, pool_scale, lru_conv_w, lru_conv_b, lru_w_r, lru_b_r,
                 lru_w_i, lru_b_i, lru_lambda, lru_w_out, sconv_w, sconv_w_out, w_mix_out, xa_w_q,
                 xa_w_k, xa_w_v, xa_w_o, ffn_w_gate, ffn_w_up, ffn_w_down, ln_g, ln_b, out):
    _, SEQ, D = x.shape
    M = mem.shape[1]
    FF = ffn_w_gate.shape[2]
    DEPTH = w_in.shape[0]
    ALPHA = (2 * DEPTH) ** 0.25
    KT = D // P
    TT = SEQ // P
    MT = M // P
    HT = FF // P
    HEADS = 4
    HD = D // HEADS
    SCORE_SCALE = float(HD) ** -0.5
    GROUPS = len(POOL_WINDOWS)
    COLS = 2048 // KT
    HALF = D // 2
    assert DEPTH == 1 and SEQ == 512 and COLS == 256 and HD == 256 and D == 1024

    A_BODY, B_BODY, F_BODY, G_BODY = 12, 20, 4, 4
    A_ITERS, B_ITERS, F_ITERS = GROUPS, KT // 4, HT // 2
    HEAD_STEPS = 6
    A0 = 0
    B0 = A0 + A_BODY * A_ITERS
    C0 = B0 + B_BODY * B_ITERS
    D0 = C0 + KT
    E0 = D0 + HEAD_STEPS * HEADS
    F0 = E0 + KT
    G0 = F0 + F_BODY * F_ITERS
    G_ITERS = (HT - 6) // G_BODY
    G_TAIL = HT - G_ITERS * G_BODY
    STEPS = G0 + HT
    POOL_STEPS = (0, 1, 2, 3)
    S_UNIT = 3

    with ExitStack() as ctx:
        def sb(name, shape, dt=F32, where=ctx):
            return where.enter_context(nc.sbuf_tensor(name, shape, dt))

        def signal(name, credit=0):
            return Signal(ctx.enter_context(nc.semaphore(name)), credit)

        ident = sb("ident", [P, P])
        par = sb("par", [P, DECAY_EXP + 1, KT])
        corr = sb("corr", [P, GROUPS, POOL_PAD])
        inv_win = sb("inv_win", [P, GROUPS])
        xT_h = sb("xT_h", [P, KT, SEQ], F32R)
        xT_l = sb("xT_l", [P, KT, SEQ], F32R)
        raw = sb("raw", [P, RAW_SLOTS, 2048])
        wh = sb("wh", [P, SPLIT_SLOTS, 1024], F32R)
        wl = sb("wl", [P, SPLIT_SLOTS, 1024], F32R)
        act32 = sb("act32", [P, KT, SEQ])

        cur = sb("cur", [P, DECAY_EXP + 1, 2])
        cur_b = sb("cur_b", [P, 3, 4])
        soft = sb("soft", [P, 8, KT])
        sums = sb("sums", [P, TT, 2])
        neg_mean = sb("neg_mean", [P, TT])
        squares = sb("squares", [P, TT])
        dev = sb("dev", [P, TT])
        eps = sb("eps", [P, 1])
        rstd = sb("rstd", [P, TT])
        row_max = sb("row_max", [P, TT])
        neg_max = sb("neg_max", [P, TT])
        row_sum = sb("row_sum", [P, TT])
        inv_sum = sb("inv_sum", [P, TT])

        with ExitStack() as scope:
            lru_h = sb("lru_h", [P, KT, SEQ], F32R, scope)
            lru_l = sb("lru_l", [P, KT, SEQ], F32R, scope)
            cnv_h = sb("cnv_h", [P, KT, SEQ], F32R, scope)
            cnv_l = sb("cnv_l", [P, KT, SEQ], F32R, scope)
        with ExitStack() as scope:
            sb("lru_first", [P, KT - 2, SEQ], F32, scope)
            u1 = sb("u1", [P, POOL_PAD + SEQ], F32, scope)
            sb("to_cnv_h", [P, (2 * KT + KT - 2) * SEQ - (KT - 2) * SEQ - (POOL_PAD + SEQ)], F32, scope)
            ra1 = sb("ra1", [P, 2, SEQ], F32, scope)
            sb("cnv_first", [P, KT - 2, SEQ], F32, scope)
            si1 = sb("si1", [P, 2, SEQ], F32, scope)
        st_h = sb("st_h", [P, SPLIT_SLOTS, SEQ], F32R)
        st_l = sb("st_l", [P, SPLIT_SLOTS, SEQ], F32R)
        gb = sb("gb", [P, 2, D])
        xnat = sb("xnat", [P, TT, D])
        kT_h = sb("kT_h", [P, 2, M], F32R)
        kT_l = sb("kT_l", [P, 2, M], F32R)
        v_h = sb("v_h", [P, 2, MT, HD], F32R)
        v_l = sb("v_l", [P, 2, MT, HD], F32R)
        qT_h = sb("qT_h", [P, 2, SEQ], F32R)
        qT_l = sb("qT_l", [P, 2, SEQ], F32R)
        probs = sb("probs", [P, TT, M])
        silu = probs[:].rearrange("p t m -> p (t m)").rearrange("p (l s) -> p l s", l=2)

        scaled = probs[:].rearrange("p t m -> p (t m)")

        with ExitStack() as scope:
            u = (sb("u", [P, POOL_PAD + SEQ], F32, scope)[:], u1[:])
            ws = (sb("ws", [P, SEQ], F32, scope)[:], act32[:, KT - 1, :])
            p_h = sb("p_h", [P, 2, SEQ], F32R, scope)
            p_l = sb("p_l", [P, 2, SEQ], F32R, scope)
            zl = sb("zl", [P, LRU_TAPS - 1 + SEQ], F32, scope)
            v = sb("v", [P, 2, SEQ], F32, scope)
            vr_h = sb("vr_h", [P, 2, SEQ], F32R, scope)
            vr_l = sb("vr_l", [P, 2, SEQ], F32R, scope)
            c = sb("c", [P, 2, SEQ], F32, scope)
            ch = sb("ch", [P, SCONV_TAPS - 1 + SEQ], F32, scope)
            o = sb("o", [P, 2, SEQ], F32, scope)
            rt = (sb("rt", [P, SEQ], F32, scope)[:], ra1[:, 0, :])
            ae = (sb("ae", [P, SEQ], F32, scope)[:], ra1[:, 1, :])
            sq = (sb("sq", [P, SEQ], F32, scope)[:], si1[:, 0, :])
            ig = (sb("ig", [P, SEQ], F32, scope)[:], si1[:, 1, :])
        with ExitStack() as scope:
            gates = sb("gates", [P, 3, 2, SEQ], F32, scope)
            memT_h = sb("memT_h", [P, KT, M], F32R, scope)
            memT_l = sb("memT_l", [P, KT, M], F32R, scope)
            mem_nat = sb("mem_nat", [P, MT, D], F32, scope)
            pT_h = sb("pT_h", [P, MT, SEQ], F32R, scope)
            pT_l = sb("pT_l", [P, MT, SEQ], F32R, scope)
        with ExitStack() as scope:
            rows = sb("rows", [P, 2, P], F32, scope)
            tok1 = sb("tok1", [P, POOL_PAD], F32, scope)
        hidden = sb("hidden", [P, HT, SEQ])

        ps = ctx.enter_context(nc.psum_tensor("ps", [P, 8, 512], F32))

        x_in = [ctx.enter_context(nc.semaphore(f"x_in{t}")) for t in range(TT)]
        rows_in = ctx.enter_context(nc.semaphore("rows_in"))
        rows_in_act = ctx.enter_context(nc.semaphore("rows_in_act"))
        first_in = ctx.enter_context(nc.semaphore("first_in"))
        raw_in = [ctx.enter_context(nc.semaphore(f"raw_in{n}")) for n in range(RAW_SLOTS)]
        small_in = ctx.enter_context(nc.semaphore("small_in"))
        mem_in = ctx.enter_context(nc.semaphore("mem_in"))
        res_in = ctx.enter_context(nc.semaphore("res_in"))
        gb_in = ctx.enter_context(nc.semaphore("gb_in"))
        stored = ctx.enter_context(nc.semaphore("stored"))
        consts = signal("consts")
        ident_set = signal("ident_set")
        iv_done = signal("iv_done", 2)
        weights_used = signal("weights_used", SPLIT_SLOTS)
        par_full = signal("par_full")
        xt_full = signal("xt_full")
        tok_full = signal("tok_full")
        scores_full = signal("scores_full")
        q_first = signal("q_first")
        pT_full = signal("pT_full")
        pv_full = signal("pv_full")
        w_hi = signal("w_hi")
        xt_hi = signal("xt_hi")
        soft_exp = signal("soft_exp")
        zl_full = signal("zl_full")
        v_tap0 = signal("v_tap0")
        vr_hi = signal("vr_hi")
        u_full = signal("u_full")
        p_hi = signal("p_hi", 2)
        c_full = signal("c_full")
        r_full = signal("r_full")
        i_full = signal("i_full", 2)
        t_full = signal("t_full")
        e_full = signal("e_full")
        sq_full = signal("sq_full")
        o_tap0 = signal("o_tap0")
        gate_full = signal("gate_full", 3)
        st_hi = signal("st_hi")
        squares_done = signal("squares_done")
        dev_full = signal("dev_full")
        kT_hi = signal("kT_hi")
        v_hi = signal("v_hi")
        q_hi = signal("q_hi")
        exp_done = signal("exp_done")
        pT_hi = signal("pT_hi")
        silu_full = signal("silu_full", 1)
        w_lo = signal("w_lo", SPLIT_SLOTS)
        xt_lo = signal("xt_lo")
        par_done = signal("par_done")
        pads = signal("pads")
        corr_step = signal("corr_step")
        soft_step = signal("soft_step")
        cur_set = signal("cur_set")
        cur_b_set = signal("cur_b_set")
        conv_step = signal("conv_step", 1)
        pool_step = signal("pool_step", 4)
        vr_lo = signal("vr_lo")
        p_lo = signal("p_lo", 1)
        ypool = signal("ypool")
        lru_step = signal("lru_step", 1)
        sconv_step = signal("sconv_step", 6)
        out_step = signal("out_step", 4)
        merge_step = signal("merge_step", 7)
        st_lo = signal("st_lo")
        res_done = signal("res_done")
        ln_step = signal("ln_step")
        kT_lo = signal("kT_lo")
        v_lo = signal("v_lo")
        q_lo = signal("q_lo")
        max_step = signal("max_step")
        norm_step = signal("norm_step")
        pT_lo = signal("pT_lo")
        ot_full = signal("ot_full")
        h_full = signal("h_full", 1)

        CONV, POOL, LRU, SCONV, OUT, LN = 3, 3, 8, 3, 3, 4

        def merge_at(pair, step, l):
            return pair * 10 + 2 * step + l

        def cols(w, first):
            return w[0].rearrange("(k p) n -> p k n", p=P)[:, :, bass.ds(first, COLS)]

        def k_rows(w, first):
            return w[0].rearrange("(k p) n -> p k n", p=P)[:, bass.ds(first, 2), :]

        LOADS = {"A": (0, 0, 3, 2), "B": (12, 8, 5, 5), "C": (22, 18, 0, 0), "D": (24, 20, 0, 0),
                 "E": (30, 26, 0, 0), "F": (32, 28, 1, 1), "G": (43, 39, 1, 1)}
        FIRST = {"A": A0, "B": B0, "C": C0, "D": D0, "E": E0, "F": F0, "G": G0}
        BODY = {"A": A_BODY, "B": B_BODY, "C": 0, "D": 0, "E": 0, "F": F_BODY, "G": G_BODY}

        def wait_raw(eng, phase, it, unit):
            per_body = BODY[phase] // 2
            if per_body and unit >= per_body:
                it, unit = it + 1, unit - per_body
            n = unit // 2 if not (phase == "A" and unit > S_UNIT) else (unit - unit % 2) // 2 - unit % 2
            before, each = LOADS[phase][unit % 2], LOADS[phase][2 + unit % 2]
            eng.wait_ge(raw_in[unit % 2], 16 * (it * each + (before + n + 1)))

        def step_no(phase, it, s):
            return it * BODY[phase] + (FIRST[phase] + s)

        def is_small(phase, s):
            return phase == "A" and s % A_BODY // 2 == S_UNIT

        def raw_part(phase, s):
            r, half = s // 2 % RAW_SLOTS, s % 2
            size = 512 if is_small(phase, s) else 1024
            return raw[:, r, half * size:(half + 1) * size], size

        def param_rows():
            def tiles(w):
                return w.rearrange("o (t p) -> (o t) p", p=P)

            loads, at = [], 0
            for w in (tiles(b_in), tiles(pool_scale), lru_conv_w[0].rearrange("k (t p) -> (k t) p", p=P),
                      tiles(lru_conv_b), tiles(lru_b_r), tiles(lru_b_i), tiles(lru_lambda),
                      sconv_w[0].rearrange("k (t p) -> (k t) p", p=P)):
                n = w.shape[0]
                loads.append((rows[at % P:at % P + n, at // P, :], w))
                at += n
            return loads

        block = ctx.enter_context(nc.Block())

        @block.sync
        def _(sp):
            def load(phase, it, unit, *copies, sem=None):
                sp.wait_ge(w_lo.sem, w_lo.done(step_no(phase, it, 2 * unit - 3)))
                for dst, src in copies:
                    sp.dma_start(dst, src).then_inc(sem or raw_in[unit % 2], 16)

            def slot(unit):
                return raw[:, unit % RAW_SLOTS, :]

            def col_slot(unit):
                return slot(unit).rearrange("p (k n) -> p k n", k=KT)

            def row_slot(unit):
                return slot(unit).rearrange("p (k n) -> p k n", k=2)

            for t in range(TT):
                sp.dma_start(act32[:].rearrange("p k s -> p (k s)")[:, t * D:(t + 1) * D],
                             x[0, t * P:(t + 1) * P, :]).then_inc(x_in[t], 16)
                if t == 1:
                    sp.dma_start(col_slot(0)[:, 0:KT // 2, :], cols(w_in, D)[:, 0:KT // 2, :]).then_inc(first_in, 16)
                if t == 2:
                    sp.dma_start(col_slot(0)[:, KT // 2:, :], cols(w_in, D)[:, KT // 2:, :]).then_inc(raw_in[0], 16)
            sp.wait_ge(x_in[TT - 1], 16)
            load("A", 0, 1, (col_slot(1), cols(w_in, 0)))

            def rest_of_a(i, c0):
                load("A", i, 2, (col_slot(2), cols(w_in, c0 + 3 * D)))
                load_small(i)
                load("A", i, 4, (col_slot(4), cols(w_in, c0 + 4 * D)))
                load("A", i, 5, (col_slot(5), cols(w_in, c0 + 2 * D)))

            def load_small(i):
                small = slot(3)
                load("A", i, S_UNIT,
                     (small[:, 0:512].rearrange("p (k n) -> p k n", k=2),
                      pool_w[0].rearrange("g (k p) n -> p (g k) n", p=P)[:, bass.ds(i * 2, 2), :]),
                     (small[:, 512:768].rearrange("p (h n) -> p h n", h=2),
                      lru_w_r[0].rearrange("h p n -> p h n")[:, bass.ds(i * 2, 2), :]),
                     (small[:, 768:1024].rearrange("p (h n) -> p h n", h=2),
                      lru_w_i[0].rearrange("h p n -> p h n")[:, bass.ds(i * 2, 2), :]),
                     sem=small_in)

            with sp.Fori(0, A_ITERS - 1) as i:
                rest_of_a(i, i * COLS)
                load("A", i, A_BODY // 2, (col_slot(0), cols(w_in, i * COLS + (D + COLS))))
                load("A", i, A_BODY // 2 + 1, (col_slot(1), cols(w_in, i * 2 * P + COLS)))
            rest_of_a(A_ITERS - 1, (A_ITERS - 1) * COLS)
            with sp.Fori(0, B_ITERS) as i:
                for q in range(2):
                    c0 = i * (2 * COLS) + q * COLS
                    for m in range(3):
                        load("B", i, 5 * q + m, (col_slot(5 * q + m), cols(w_in, c0 + (5 + m) * D)))
                    load("B", i, 5 * q + 3, (col_slot(5 * q + 3), cols(lru_w_out, i * 4 * P + q * COLS)))
                    load("B", i, 5 * q + 4, (col_slot(5 * q + 4), cols(sconv_w_out, i * 4 * P + q * COLS)))
            for n in range(KT // 2):
                load("C", 0, n, (row_slot(n), k_rows(w_mix_out, 2 * n)))
            for h in range(HEADS):
                for n, w in enumerate((xa_w_k, xa_w_v, xa_w_q)):
                    load("D", 0, 3 * h + n, (col_slot(3 * h + n), cols(w, h * HD)))
            for n in range(KT // 2):
                load("E", 0, n, (row_slot(n), k_rows(xa_w_o, 2 * n)))
            with sp.Fori(0, F_ITERS) as i:
                load("F", i, 0, (col_slot(0), cols(ffn_w_gate, i * COLS)))
                load("F", i, 1, (col_slot(1), cols(ffn_w_up, i * 2 * P)))
            with sp.Fori(0, G_ITERS) as i:
                load("G", i, 0, (row_slot(0), k_rows(ffn_w_down, i * 4)))
                load("G", i, 1, (row_slot(1), k_rows(ffn_w_down, i * 4 + 2)))
            for n in range(2 * G_ITERS, HT // 2):
                load("G", 0, n, (row_slot(n), k_rows(ffn_w_down, 2 * n)))
            for t in range(TT):
                for n, part in enumerate((slice(0, HALF), slice(HALF, D)) if t == TT - 1 else (slice(0, D),)):
                    sp.wait_ge(ln_step.sem, ln_step.done(LN * (2 * TT + t) + 3 + n))
                    sp.dma_start(out[0, t * P:(t + 1) * P, part], xnat[:, t, part]).then_inc(stored, 16)
            sp.wait_ge(stored, 16 * (TT + 1))

        @block.gpsimd
        def _(pool):
            nc.gpsimd.memset(ident[:], 0.0).then_inc(ident_set.sem, 1)
            pool.wait_ge(ident_set.sem, ident_set.done(0))
            nc.gpsimd.affine_select(out=ident[:], in_=ident[:], compare_op=ALU.not_equal, fill=1.0, base=0,
                                    pattern=[[-1, P]], channel_multiplier=1).then_inc(consts.sem, 1)
            nc.gpsimd.iota(tok1[:], pattern=[[1, POOL_PAD]], base=1, channel_multiplier=0,
                           allow_small_or_imprecise_dtypes=True).then_inc(consts.sem, 1)
            for dst, src in param_rows()[3:]:
                pool.dma_start(dst, src).then_inc(rows_in, 16)

            def split(n):
                pool.wait_ge(w_hi.sem, w_hi.done(n))
                pool.wait_ge(w_lo.sem, w_lo.done(n - 1))
                src = raw[:, n // 2 % RAW_SLOTS, n % 2 * 1024:(n % 2 + 1) * 1024]
                nc.gpsimd.tensor_tensor(wl[:, n % SPLIT_SLOTS, :], src, wh[:, n % SPLIT_SLOTS, :].bitcast(F32),
                                        ALU.subtract).then_inc(w_lo.sem, 1)

            split(A0)
            pool.sem_inc(iv_done.sem, iv_done.credit)
            with pool.Fori(0, A_ITERS) as i:
                for l in range(2):
                    j = i * 2 + l
                    pool.wait_ge(conv_step.sem, conv_step.done(j * CONV + 2))
                    pool.wait_ge(i_full.sem, i_full.done(j))
                    nc.gpsimd.tensor_tensor(ig[l], ig[l], v[:, l, :], ALU.mult).then_inc(iv_done.sem, 1)
            pool.wait_ge(lru_step.sem, lru_step.done(LRU * KT - 1))
            pool.wait_ge(out_step.sem, out_step.done(OUT * KT - 1))
            pool.dma_start(mem_nat[:], mem[0].rearrange("(t p) d -> p t d", p=P)).then_inc(mem_in, 16)
            pool.wait_ge(weights_used.sem, weights_used.done(C0 - 1))
            pool.dma_start(xnat[:], x[0].rearrange("(t p) d -> p t d", p=P)).then_inc(res_in, 16)

            def load_gb(n):
                pool.dma_start(gb[:, 0, :], ln_g[0, n:n + 1, :].broadcast_to([P, D])).then_inc(gb_in, 16)
                pool.dma_start(gb[:, 1, :], ln_b[0, n:n + 1, :].broadcast_to([P, D])).then_inc(gb_in, 16)

            load_gb(0)
            for n in POOL_STEPS:
                split(D0 + n)
            pool.wait_ge(ln_step.sem, ln_step.done(LN * TT - 1))
            load_gb(1)
            for n in POOL_STEPS:
                split(F0 + n)
            pool.wait_ge(ln_step.sem, ln_step.done(LN * 2 * TT - 1))
            load_gb(2)

        @block.tensor
        def _(pe):
            def mm3(dst, st, st_lo_part, mv_, mv_lo_part, start, stop):
                nc.tensor.matmul(dst, st, mv_, start=start, stop=False)
                nc.tensor.matmul(dst, st, mv_lo_part, start=False, stop=False)
                return nc.tensor.matmul(dst, st_lo_part, mv_, start=False, stop=stop)

            def weights_ready(phase, it, s):
                pe.wait_ge(w_lo.sem, w_lo.done(step_no(phase, it, s)))

            def col_unit(phase, it, unit, bank, mh, ml, width=SEQ, first=None):
                for half in range(2):
                    s = 2 * unit + half
                    weights_ready(phase, it, s)
                    h_, l_ = (w[:, s % SPLIT_SLOTS, :].rearrange("p (k n) -> p k n", k=4) for w in (wh, wl))
                    for l in range(2):
                        for k in range(4):
                            last = mm3(ps[:, bank + l, 0:width],
                                       h_[:, k, l * P:(l + 1) * P], l_[:, k, l * P:(l + 1) * P],
                                       mh[:, 4 * half + k, :], ml[:, 4 * half + k, :],
                                       half == 0 and k == 0, half == 1 and k == 3)
                        if first and half == 1 and l == 0:
                            last.then_inc(first.sem, 1)
                    last.then_inc(weights_used.sem, 1)

            def turn(src, tile, bank, width=4):
                for half in range(2):
                    for n in range(width):
                        k = 4 * half + n
                        last = nc.tensor.transpose(ps[:, bank + half, n * P:(n + 1) * P],
                                                   src[:, tile, k * P:(k + 1) * P], ident[:])
                    last.then_inc(xt_full.sem, 1)

            pe.sem_inc(weights_used.sem, weights_used.credit)
            pe.wait_ge(consts.sem, consts.done(0))
            x_nat0 = act32[:].rearrange("p k s -> p (k s)").rearrange("p (t d) -> p t d", t=TT)

            def keep_busy(n):
                for _ in range(n):
                    nc.tensor.transpose(ps[:, 7, 0:P], ident[:], ident[:])

            keep_busy(14)
            def turn_x(t):
                pe.wait_ge(x_in[t], 16)
                turn(x_nat0, t, 2 * t)

            for t in range(TT - 1):
                turn_x(t)
                keep_busy(4)

            def half_tokens(phase, unit, bank, part, between):
                tokens = slice(part * SEQ // 2, (part + 1) * SEQ // 2)
                for half in range(2):
                    s = 2 * unit + half
                    if part == 0:
                        weights_ready(phase, 0, s)
                    h_, l_ = (w[:, s, :].rearrange("p (k n) -> p k n", k=4) for w in (wh, wl))
                    for l in range(2):
                        for k in range(4):
                            kk = 4 * half + k
                            last = mm3(ps[:, bank + l, tokens],
                                       h_[:, k, l * P:(l + 1) * P], l_[:, k, l * P:(l + 1) * P],
                                       xT_h[:, kk, tokens], xT_l[:, kk, tokens], kk == 0, kk == KT - 1)
                    if part == 1:
                        last.then_inc(weights_used.sem, 1)
                    if (part, s) in between:
                        between[(part, s)]()

            def a_pass(i, first=False):
                j1 = i * 2 + 1
                if first:
                    pe.wait_ge(xt_lo.sem, xt_lo.done(3))
                    half_tokens("A", 0, 0, 0, {(0, 0): lambda: turn_x(TT - 1)})
                    pe.wait_ge(xt_lo.sem, xt_lo.done(2 * TT - 1))
                    pe.wait_ge(rows_in_act, 3 * 16)
                    pe.wait_ge(rows_in, 5 * 16)
                    nc.tensor.transpose(ps[:, 7, 0:P], rows[:, 0, :], ident[:])
                    nc.tensor.transpose(ps[:, 7, P:P + 32], rows[0:32, 1, :],
                                        ident[0:32, 0:32]).then_inc(par_full.sem, 1)
                    half_tokens("A", 0, 0, 1, {})
                else:
                    pe.wait_ge(i_full.sem, i_full.done(i * 2 - 2))
                    col_unit("A", i, 0, 0, xT_h, xT_l)
                pe.wait_ge(i_full.sem, i_full.done(i * 2 - 1))
                col_unit("A", i, 1, 2, xT_h, xT_l)
                pe.wait_ge(sconv_step.sem, sconv_step.done(i * (2 * SCONV) - SCONV))
                col_unit("A", i, 2, 4, xT_h, xT_l)
                weights_ready("A", i, 6)
                pe.wait_ge(p_lo.sem, p_lo.done(j1))
                pe.wait_ge(par_done.sem, par_done.done(0))
                pe.wait_ge(out_step.sem, out_step.done(i * (2 * OUT) - OUT))
                h_, l_ = (w[:, 2, 0:512].rearrange("p (k n) -> p k n", k=2) for w in (wh, wl))
                for l in range(2):
                    for k in range(2):
                        last = mm3(ps[:, 6 + l, :], h_[:, k, l * P:(l + 1) * P], l_[:, k, l * P:(l + 1) * P],
                                   p_h[:, k, :], p_l[:, k, :], k == 0, k == 1)
                last.then_inc(weights_used.sem, 1)
                weights_ready("A", i, 7)
                pe.wait_ge(vr_lo.sem, vr_lo.done(j1))
                pe.wait_ge(u_full.sem, u_full.done(j1))
                for l in range(2):
                    for g in range(2):
                        at = (2 * g + l) * P
                        last = mm3(ps[:, 2 * l + g, :], wh[:, 3, at:at + P], wl[:, 3, at:at + P],
                                   vr_h[:, l, :], vr_l[:, l, :], True, True)
                last.then_inc(weights_used.sem, 1)
                pe.wait_ge(c_full.sem, c_full.done(j1))
                col_unit("A", i, 4, 4, xT_h, xT_l)
                pe.wait_ge(ypool.sem, ypool.done(j1))
                col_unit("A", i, 5, 6, xT_h, xT_l)

            a_pass(0, first=True)
            with pe.Fori(1, A_ITERS) as i:
                a_pass(i)

            with pe.Fori(0, B_ITERS) as i:
                pe.wait_ge(i_full.sem, i_full.done(KT - 2))
                pe.wait_ge(merge_step.sem, merge_step.done(i * 20 + (merge_at(-1, 1, 1))))
                col_unit("B", i, 0, 0, xT_h, xT_l)
                pe.wait_ge(i_full.sem, i_full.done(KT - 1))
                pe.wait_ge(merge_step.sem, merge_step.done(i * 20 + (merge_at(-1, 3, 1))))
                col_unit("B", i, 1, 2, xT_h, xT_l)
                pe.wait_ge(sconv_step.sem, sconv_step.done(SCONV * (KT - 1)))
                pe.wait_ge(gate_full.sem, gate_full.done(i * 12 - 3))
                col_unit("B", i, 2, 4, xT_h, xT_l)
                pe.wait_ge(out_step.sem, out_step.done(OUT * KT - 1))
                pe.wait_ge(gate_full.sem, gate_full.done(i * 12 - 1))
                pe.wait_ge(lru_step.sem, lru_step.done(LRU * KT - 1))
                col_unit("B", i, 3, 6, lru_h, lru_l)
                pe.wait_ge(gate_full.sem, gate_full.done(i * 12 + 1))
                col_unit("B", i, 4, 0, cnv_h, cnv_l)
                pe.wait_ge(gate_full.sem, gate_full.done(i * 12 + 3))
                col_unit("B", i, 5, 2, xT_h, xT_l)
                pe.wait_ge(gate_full.sem, gate_full.done(i * 12 + 5))
                col_unit("B", i, 6, 4, xT_h, xT_l)
                pe.wait_ge(merge_step.sem, merge_step.done(i * 20 + merge_at(0, 1, 1)))
                col_unit("B", i, 7, 6, xT_h, xT_l)
                pe.wait_ge(merge_step.sem, merge_step.done(i * 20 + merge_at(0, 3, 1)))
                col_unit("B", i, 8, 0, lru_h, lru_l)
                pe.wait_ge(gate_full.sem, gate_full.done(i * 12 + 7))
                col_unit("B", i, 9, 2, cnv_h, cnv_l)

            pe.wait_ge(mem_in, 16)
            pe.wait_ge(gate_full.sem, gate_full.done(6 * (KT // 2) - 1))
            for t in range(MT):
                turn(mem_nat, t, 4 + 2 * t)

            def accumulate_half(slot, bank, t, half, start, stop):
                return mm3(ps[:, bank + half, :],
                           st_h[:, slot, t * P:(t + 1) * P], st_l[:, slot, t * P:(t + 1) * P],
                           wh[:, slot, half * HALF:(half + 1) * HALF], wl[:, slot, half * HALF:(half + 1) * HALF],
                           start, stop)

            def accumulate(slot, bank, t, start, stop):
                for half in range(2):
                    last = accumulate_half(slot, bank, t, half, start, stop)
                return last

            def k_ready(phase, it, s, stage):
                weights_ready(phase, it, s)
                pe.wait_ge(st_lo.sem, st_lo.done(stage))

            def k_outer(phase, it, s, stage, start):
                k_ready(phase, it, s, stage)
                for t in range(TT):
                    last = accumulate(s % SPLIT_SLOTS, 2 * t, t, start, False)
                last.then_inc(weights_used.sem, 1)

            def turn_next(phase, t):
                pe.wait_ge(ln_step.sem, ln_step.done(LN * ((0 if phase == "C" else TT) + t) + 3))
                turn(xnat, t, 2 * t if phase == "C" else e_bank(t))

            def e_bank(t):
                return (2 * t + 2) % 8

            def last_four(phase, s0, stage0, t, bank):
                if phase == "G" and t == TT - 1:
                    for half in range(2):
                        for n in range(4):
                            last = accumulate_half((s0 + n) % SPLIT_SLOTS, bank, t, half, False, n == 3)
                        if half == 0:
                            last.then_inc(tok_full.sem, 1)
                    last.then_inc(weights_used.sem, 1)
                    return
                for n in range(4):
                    if n == 2 and t >= 2 and phase != "G":
                        turn_next(phase, t - 2)
                    if t == 0:
                        k_ready(phase, 0, s0 + n, stage0 + n)
                    last = accumulate((s0 + n) % SPLIT_SLOTS, bank, t, False, n == 3)
                    if t == TT - 1:
                        last.then_inc(weights_used.sem, 1)
                if t < TT - 1:
                    last.then_inc(tok_full.sem, 1)

            for k in range(4):
                k_ready("C", 0, k, k)
                for t in range(TT):
                    if k == 0 and t == 0:
                        pe.wait_ge(merge_step.sem, merge_step.done(merge_at(KT // 2 - 1, 1, 1)))
                    if k == 0 and t == 1:
                        pe.wait_ge(merge_step.sem, merge_step.done(merge_at(KT // 2 - 1, 3, 1)))
                    if k == 0 and t >= 2:
                        pe.wait_ge(xt_lo.sem, xt_lo.done(8 + 2 * (t - 2) + 1))
                    last = accumulate(k, 2 * t, t, k == 0, False)
                last.then_inc(weights_used.sem, 1)
            for t in range(TT):
                last_four("C", 4, 4, t, 2 * t)

            def turn_probs(h):
                pe.wait_ge(norm_step.sem, norm_step.done(5 * h + 4))
                for m in range(MT):
                    for t in range(TT):
                        last = nc.tensor.transpose(ps[:, 6 + m, t * P:(t + 1) * P],
                                                   probs[:, t, m * P:(m + 1) * P], ident[:])
                    last.then_inc(pT_full.sem, 1)

            def weigh_values(h):
                pe.wait_ge(pT_lo.sem, pT_lo.done(MT * h + 1))
                for d in range(2):
                    for m in range(MT):
                        last = mm3(ps[:, d, :], v_h[:, h % 2, m, d * P:(d + 1) * P], v_l[:, h % 2, m, d * P:(d + 1) * P],
                                   pT_h[:, m, :], pT_l[:, m, :], m == 0, m == MT - 1)
                    last.then_inc(pv_full.sem, 1)

            for h in range(HEADS):
                if h == 0:
                    pe.wait_ge(xt_lo.sem, xt_lo.done(12 + 1))
                elif h > 1:
                    pe.wait_ge(ot_full.sem, ot_full.done(2 * (h - 2) + 1))
                else:
                    pe.wait_ge(kT_lo.sem, kT_lo.done(1))
                pe.wait_ge(xt_lo.sem, xt_lo.done(8 + 3))
                col_unit("D", 0, 3 * h, 0, memT_h, memT_l, M)
                if h == 0:
                    turn_next("C", 2)
                    pe.wait_ge(xt_lo.sem, xt_lo.done(12 + 3))
                else:
                    pe.wait_ge(v_lo.sem, v_lo.done(MT * h - 1))
                for half in range(2):
                    s = 2 * (3 * h + 1) + half
                    if h == 0 and half == 1:
                        turn_next("C", 3)
                    weights_ready("D", 0, s)
                    h_, l_ = (w[:, s % SPLIT_SLOTS, :].rearrange("p (k n) -> p k n", k=4) for w in (wh, wl))
                    for m in range(MT):
                        for k in range(4):
                            kk = 4 * half + k
                            last = mm3(ps[:, 2 + m, 0:HD],
                                       memT_h[:, kk, m * P:(m + 1) * P], memT_l[:, kk, m * P:(m + 1) * P],
                                       h_[:, k, :], l_[:, k, :], kk == 0, kk == KT - 1)
                    last.then_inc(weights_used.sem, 1)
                if h == 0:
                    pe.wait_ge(xt_lo.sem, xt_lo.done(12 + 7))
                else:
                    turn_probs(h - 1)
                    pe.wait_ge(q_lo.sem, q_lo.done(2 * h - 1))
                col_unit("D", 0, 3 * h + 2, 4, xT_h, xT_l, first=q_first)
                if h:
                    pe.wait_ge(kT_lo.sem, kT_lo.done(2 * h + 1))
                    weigh_values(h - 1)
                pe.wait_ge(kT_lo.sem, kT_lo.done(2 * h + 1))
                for b in range(2):
                    for t in (2 * b, 2 * b + 1):
                        for d in range(2):
                            if t == 0:
                                pe.wait_ge(q_lo.sem, q_lo.done(2 * h + d))
                            last = mm3(ps[:, 6 + b, t % 2 * M:(t % 2 + 1) * M],
                                       qT_h[:, d, t * P:(t + 1) * P], qT_l[:, d, t * P:(t + 1) * P],
                                       kT_h[:, d, :], kT_l[:, d, :], d == 0, d == 1)
                    last.then_inc(scores_full.sem, 1)

            def first_pair(k):
                k_ready("E", 0, k, KT + k)
                for t in range(2):
                    accumulate(k, e_bank(t), t, k == 0, False)

            pe.wait_ge(v_lo.sem, v_lo.done(MT * HEADS - 1))
            pe.wait_ge(q_lo.sem, q_lo.done(2 * HEADS - 1))
            first_pair(0)
            first_pair(1)
            turn_probs(HEADS - 1)
            first_pair(2)
            first_pair(3)
            pe.wait_ge(ot_full.sem, ot_full.done(2 * HEADS - 3))
            weigh_values(HEADS - 1)
            pe.wait_ge(pT_lo.sem, pT_lo.done(MT * HEADS - 1))
            for k, t in ((0, 2), (1, 2), (0, 3), (1, 3), (2, 2), (2, 3), (3, 2), (3, 3)):
                if (k, t) == (0, 3):
                    pe.wait_ge(ot_full.sem, ot_full.done(2 * HEADS - 1))
                last = accumulate(k, e_bank(t), t, k == 0, False)
                if t == 3:
                    last.then_inc(weights_used.sem, 1)
            for t in range(TT):
                last_four("E", 4, KT + 4, t, e_bank(t))

            turns = {(0, 1): lambda: turn_next("E", 2), (0, 2): lambda: turn_next("E", 3)}
            for part in range(2):
                pe.wait_ge(xt_lo.sem, xt_lo.done(20 + 4 * part + 3))
                for unit in range(2):
                    half_tokens("F", unit, 2 + 2 * unit, part, turns)
            with pe.Fori(1, F_ITERS) as i:
                pe.wait_ge(silu_full.sem, silu_full.done(i * 2 - 1))
                col_unit("F", i, 0, 0, xT_h, xT_l)
                pe.wait_ge(h_full.sem, h_full.done(i * 2 - 1))
                col_unit("F", i, 1, 2, xT_h, xT_l)

            for k in range(G_BODY):
                k_ready("G", 0, k, 2 * KT + k)
                for t in (2, 3, 0, 1):
                    if k == 0 and t == 0:
                        pe.wait_ge(silu_full.sem, silu_full.done(HT - 1))
                    if k == 0 and t == 1:
                        pe.wait_ge(h_full.sem, h_full.done(HT - 1))
                    last = accumulate(k, 2 * t, t, k == 0, False)
                last.then_inc(weights_used.sem, 1)
            with pe.Fori(1, G_ITERS) as i:
                for k in range(G_BODY):
                    k_outer("G", i, k, i * G_BODY + (2 * KT + k), False)
            for k in range(G_ITERS * G_BODY, HT - 4):
                k_outer("G", 0, k, 2 * KT + k, False)
            for t in range(TT):
                last_four("G", HT - 4, 2 * KT + HT - 4, t, 2 * t)

        @block.scalar
        def _(act):
            def split(phase, it, s):
                s += LOOKAHEAD
                act.wait_ge(weights_used.sem, weights_used.done(step_no(phase, it, s - SPLIT_SLOTS)))
                if is_small(phase, s):
                    act.wait_ge(small_in, 48 * (it + 1))
                elif s % 2 == 0:
                    wait_raw(act, phase, it, s // 2)
                src, size = raw_part(phase, s)
                nc.scalar.activation(wh[:, s % SPLIT_SLOTS, 0:size], src, ACT.Copy).then_inc(w_hi.sem, 1)

            def turned(first, t, bank, dst, width):
                for half in range(2):
                    act.wait_ge(xt_full.sem, xt_full.done(first + half))
                    nc.scalar.activation(dst[:, 4 * half:4 * half + 4, t * P:(t + 1) * P],
                                         ps[:, bank + half, :].rearrange("p (k q) -> p k q", k=4),
                                         ACT.Copy).then_inc(xt_hi.sem, 1)

            def stage(source_ready, src, n, slot):
                source_ready()
                nc.scalar.activation(st_h[:, slot, :], src, ACT.Copy).then_inc(st_hi.sem, 1)

            def stage_c(k):
                stage(lambda: act.wait_ge(merge_step.sem, merge_step.done(merge_at(k // 2, 4, k % 2))),
                      act32[:, k, :], k, k % SPLIT_SLOTS)

            def stage_e(k):
                stage(lambda: act.wait_ge(ot_full.sem, ot_full.done(k)), act32[:, k, :], k, k % SPLIT_SLOTS)

            def deviation(n, t, bank):
                tile = n * TT + t
                act.wait_ge(ln_step.sem, ln_step.done(LN * tile))
                nc.scalar.activation(ps[:, bank:bank + 2, :].rearrange("p b n -> p (b n)"), xnat[:, t, :],
                                     ACT.Square, bias=neg_mean[:, t:t + 1],
                                     accum_out=squares[:, t:t + 1]).then_inc(squares_done.sem, 1)
                act.wait_ge(squares_done.sem, squares_done.done(tile))
                nc.scalar.activation(dev[:, t:t + 1], squares[:, t:t + 1], ACT.Sqrt, scale=1.0 / D,
                                     bias=eps[:]).then_inc(dev_full.sem, 1)

            for s in (p_hi, i_full, gate_full, silu_full):
                act.sem_inc(s.sem, s.credit)
            for dst, src in param_rows()[:3]:
                act.dma_start(dst, src).then_inc(rows_in_act, 16)
            for t in range(TT):
                turned(2 * t, t, 2 * t, xT_h, P)
                if t == 0:
                    act.wait_ge(first_in, 16)
                    nc.scalar.activation(wh[:, 0, :], raw[:, 0, 0:1024], ACT.Copy).then_inc(w_hi.sem, 1)
                if t == 2:
                    wait_raw(act, "A", 0, 0)
                    nc.scalar.activation(wh[:, 1, :], raw[:, 0, 1024:2048], ACT.Copy).then_inc(w_hi.sem, 1)
            split("A", 0, -1)
            act.wait_ge(soft_step.sem, soft_step.done(1))
            nc.scalar.activation(soft[:, 2, :], soft[:, 1, :], ACT.Exp).then_inc(soft_exp.sem, 1)

            def gate_chains(i):
                act.wait_ge(weights_used.sem, weights_used.done(step_no("A", i, 7)))
                act.wait_ge(lru_step.sem, lru_step.done(i * (2 * LRU) - 1))
                for l in range(2):
                    nc.scalar.activation(rt[l], ps[:, 2 * l, :], ACT.Sigmoid,
                                         bias=cur[:, RATE_R_B, l:l + 1]).then_inc(r_full.sem, 1)
                    nc.scalar.activation(ig[l], ps[:, 2 * l + 1, :], ACT.Sigmoid,
                                         bias=cur[:, RATE_I_B, l:l + 1]).then_inc(i_full.sem, 1)
                for l in range(2):
                    act.wait_ge(r_full.sem, r_full.done(i * 2 + l))
                    nc.scalar.activation(ae[l], rt[l], ACT.Exp,
                                         scale=cur[:, DECAY_EXP, l:l + 1]).then_inc(e_full.sem, 1)
                for l in range(2):
                    act.wait_ge(e_full.sem, e_full.done(i * 2 + l))
                    nc.scalar.activation(rt[l], rt[l], ACT.Tanh,
                                         scale=cur[:, DECAY, l:l + 1]).then_inc(t_full.sem, 1)
                for l in range(2):
                    act.wait_ge(lru_step.sem, lru_step.done(i * (2 * LRU) + l))
                    nc.scalar.activation(sq[l], sq[l], ACT.Sqrt).then_inc(sq_full.sem, 1)

            split("A", 0, 0)
            with act.Fori(0, A_ITERS) as i:
                for s in range(A_BODY):
                    if s:
                        split("A", i, s)
                    if s in (2, 3):
                        l = s - 2
                        j = i * 2 + l
                        if l == 0:
                            act.wait_ge(cur_set.sem, cur_set.done(i))
                        act.wait_ge(weights_used.sem, weights_used.done(step_no("A", i, 1)))
                        act.wait_ge(conv_step.sem, conv_step.done(j * CONV - 1))
                        nc.scalar.activation(zl[:, LRU_TAPS - 1:], ps[:, l, :], ACT.Identity,
                                             bias=cur[:, B_LRU, l:l + 1]).then_inc(zl_full.sem, 1)
                        act.wait_ge(zl_full.sem, zl_full.done(j))
                        act.wait_ge(iv_done.sem, iv_done.done(j - 2))
                        nc.scalar.activation(v[:, l, :], zl[:, 0:SEQ], ACT.Identity,
                                             scale=cur[:, LRU_W0, l:l + 1],
                                             bias=cur[:, LRU_B, l:l + 1]).then_inc(v_tap0.sem, 1)
                    if s in (3, 4):
                        j = i * 2 + (s - 3)
                        act.wait_ge(conv_step.sem, conv_step.done(j * CONV + 2))
                        nc.scalar.activation(vr_h[:, s - 3, :], v[:, s - 3, :], ACT.Copy).then_inc(vr_hi.sem, 1)
                    if s == 4:
                        act.wait_ge(weights_used.sem, weights_used.done(step_no("A", i, 3)))
                        for l in range(2):
                            j = i * 2 + l
                            act.wait_ge(pool_step.sem, pool_step.done(j * POOL - 4))
                            nc.scalar.activation(u[l][:, POOL_PAD:], ps[:, 2 + l, :], ACT.Identity,
                                                 bias=cur[:, B_POOL, l:l + 1]).then_inc(u_full.sem, 1)
                        for l in range(2):
                            j = i * 2 + l
                            act.wait_ge(pool_step.sem, pool_step.done(j * POOL + 2))
                            nc.scalar.activation(p_h[:, l, :], ws[l], ACT.Copy).then_inc(p_hi.sem, 1)
                    if s in (6, 7):
                        l = s - 6
                        j = i * 2 + l
                        act.wait_ge(weights_used.sem, weights_used.done(step_no("A", i, 5)))
                        act.wait_ge(sconv_step.sem, sconv_step.done(j * SCONV - 2 * SCONV))
                        nc.scalar.activation(c[:, l, :], ps[:, 4 + l, :], ACT.Identity,
                                             bias=cur[:, B_C, l:l + 1]).then_inc(c_full.sem, 1)
                    if s == 8:
                        gate_chains(i)
                    if s in (10, 11):
                        l = s - 10
                        j = i * 2 + l
                        act.wait_ge(sconv_step.sem, sconv_step.done(j * SCONV))
                        act.wait_ge(out_step.sem, out_step.done(j * OUT - (2 * OUT - 2)))
                        nc.scalar.activation(o[:, l, :], ch[:, 0:SEQ], ACT.Identity,
                                             scale=cur[:, SC_W0, l:l + 1]).then_inc(o_tap0.sem, 1)
                split("A", i, A_BODY)

            def b_pass(i, last=False):
                for s in range(B_BODY):
                    if s:
                        split("B", i, s)
                    q, at = s // 10, s % 10
                    if at in (2, 4, 6):
                        m = at // 2 - 1
                        if s == 2:
                            act.wait_ge(cur_b_set.sem, cur_b_set.done(i))
                        act.wait_ge(weights_used.sem, weights_used.done(step_no("B", i, s - 1)))
                        act.wait_ge(merge_step.sem, merge_step.done(i * 20 + merge_at(q - 1, 4, 1)))
                        for l in range(2):
                            nc.scalar.activation(gates[:, m, l, :], ps[:, (0, 2)[q] + 2 * m + l, :], ACT.Sigmoid,
                                                 bias=cur_b[:, m, 2 * q + l:2 * q + l + 1]).then_inc(gate_full.sem, 1)
                if not last:
                    split("B", i, B_BODY)

            with act.Fori(0, B_ITERS - 1) as i:
                b_pass(i)
            b_pass(B_ITERS - 1, last=True)

            for k in range(LOOKAHEAD):
                if k == 0:
                    act.wait_ge(weights_used.sem, weights_used.done(C0 - 3))
                stage_c(k)
            for t in range(MT):
                turned(8 + 2 * t, t, 4 + 2 * t, memT_h, P)
            for s in range(5):
                split("C", 0, s)
                stage_c(s + LOOKAHEAD)
            deviation(0, 0, 0)
            deviation(0, 1, 2)
            turned(12, 0, 0, xT_h, P)
            split("C", 0, 5)
            deviation(0, 2, 4)
            split("C", 0, 6)
            turned(14, 1, 2, xT_h, P)
            split("C", 0, 7)
            split("D", 0, 0)
            deviation(0, 3, 6)

            def exps(h):
                for t in range(TT):
                    act.wait_ge(max_step.sem, max_step.done(4 * h + 2 * (t // 2) + 1))
                    nc.scalar.activation(probs[:, t, :], ps[:, 6 + t // 2, t % 2 * M:(t % 2 + 1) * M], ACT.Exp,
                                         scale=SCORE_SCALE, bias=neg_max[:, t:t + 1],
                                         accum_out=row_sum[:, t:t + 1]).then_inc(exp_done.sem, 1)

            def probs_hi(h):
                for m in range(MT):
                    act.wait_ge(pT_full.sem, pT_full.done(MT * h + m))
                    nc.scalar.activation(pT_h[:, m, :], ps[:, 6 + m, :], ACT.Copy).then_inc(pT_hi.sem, 1)

            for h in range(HEADS):
                base = HEAD_STEPS * h
                for s in range(HEAD_STEPS):
                    if h or s > 2:
                        split("D", 0, base + s)
                    if s == 2:
                        act.wait_ge(weights_used.sem, weights_used.done(D0 + base + 1))
                        for d in range(2):
                            nc.scalar.activation(kT_h[:, d, :], ps[:, d, 0:M], ACT.Copy).then_inc(kT_hi.sem, 1)
                        if h == 0:
                            turned(16, 2, 4, xT_h, P)
                            split("D", 0, 1)
                            split("D", 0, 2)
                            turned(18, 3, 6, xT_h, P)
                    if s == 4:
                        act.wait_ge(weights_used.sem, weights_used.done(D0 + base + 3))
                        for m in range(MT):
                            nc.scalar.activation(v_h[:, h % 2, m, :], ps[:, 2 + m, 0:HD], ACT.Copy).then_inc(v_hi.sem, 1)
                        if h:
                            probs_hi(h - 1)
                if h == HEADS - 1:
                    for k in range(4):
                        stage_e(k)
                for d in range(2):
                    if d == 0:
                        act.wait_ge(q_first.sem, q_first.done(h))
                    else:
                        act.wait_ge(weights_used.sem, weights_used.done(D0 + base + 5))
                    nc.scalar.activation(qT_h[:, d, :], ps[:, 4 + d, :], ACT.Copy).then_inc(q_hi.sem, 1)
                if h == HEADS - 1:
                    split("E", 0, 0)
                exps(h)
            probs_hi(HEADS - 1)

            for s in range(1, 5):
                split("E", 0, s)
                stage_e(s + LOOKAHEAD)
            deviation(1, 0, 2)
            deviation(1, 1, 4)
            turned(20, 0, 2, xT_h, P)
            split("E", 0, 5)
            deviation(1, 2, 6)
            turned(22, 1, 4, xT_h, P)
            split("E", 0, 6)
            split("E", 0, 7)
            split("F", 0, 0)
            deviation(1, 3, 0)
            turned(24, 2, 6, xT_h, P)
            turned(26, 3, 0, xT_h, P)

            def gate_and_up(i, first=0, bank=0):
                for s in range(first, F_BODY):
                    split("F", i, s)
                    if s == 2:
                        act.wait_ge(weights_used.sem, weights_used.done(step_no("F", i, 1)))
                        act.wait_ge(h_full.sem, h_full.done(i * 2 - 1))
                        for l in range(2):
                            nc.scalar.activation(silu[:, l, :], ps[:, bank + l, :], ACT.Silu).then_inc(silu_full.sem, 1)

            gate_and_up(0, 1, 2)
            with act.Fori(1, F_ITERS) as i:
                gate_and_up(i)

            act.wait_ge(h_full.sem, h_full.done(LOOKAHEAD - 1))
            for k in range(LOOKAHEAD):
                nc.scalar.activation(st_h[:, k, :], hidden[:, k, :], ACT.Copy).then_inc(st_hi.sem, 1)
            with act.Fori(0, G_ITERS) as i:
                for s in range(G_BODY):
                    split("G", i, s)
                    nc.scalar.activation(st_h[:, (s + LOOKAHEAD) % SPLIT_SLOTS, :],
                                         hidden[:, i * G_BODY + (s + LOOKAHEAD), :], ACT.Copy).then_inc(st_hi.sem, 1)
            for s in range(G_ITERS * G_BODY, HT - LOOKAHEAD):
                split("G", 0, s)
                nc.scalar.activation(st_h[:, (s + LOOKAHEAD) % SPLIT_SLOTS, :],
                                     hidden[:, s + LOOKAHEAD, :], ACT.Copy).then_inc(st_hi.sem, 1)
            for t in range(TT):
                deviation(2, t, 2 * t)

        @block.vector
        def _(dve):
            def split(phase, it, s):
                s += LOOKAHEAD
                dve.wait_ge(w_hi.sem, w_hi.done(step_no(phase, it, s)))
                src, size = raw_part(phase, s)
                slot = s % SPLIT_SLOTS
                nc.vector.tensor_tensor(wl[:, slot, 0:size], src, wh[:, slot, 0:size].bitcast(F32),
                                        ALU.subtract).then_inc(w_lo.sem, 1)

            def turned(first, t, bank, dst_h, dst):
                for half in range(2):
                    part = (slice(None), slice(4 * half, 4 * half + 4), slice(t * P, (t + 1) * P))
                    dve.wait_ge(xt_hi.sem, xt_hi.done(first + half))
                    nc.vector.tensor_tensor(dst[part], ps[:, bank + half, :].rearrange("p (k q) -> p k q", k=4),
                                            dst_h[part].bitcast(F32), ALU.subtract).then_inc(xt_lo.sem, 1)

            def stage(src, n, slot):
                dve.wait_ge(st_hi.sem, st_hi.done(n))
                nc.vector.tensor_tensor(st_l[:, slot, :], src, st_h[:, slot, :].bitcast(F32),
                                        ALU.subtract).then_inc(st_lo.sem, 1)

            def layer_norm(n, t, bank, meanwhile=None):
                tile = n * TT + t
                last_one = tile == 3 * TT - 1
                if t < TT - 1 or last_one:
                    dve.wait_ge(tok_full.sem, tok_full.done(n * (TT - 1) + t))
                else:
                    dve.wait_ge(weights_used.sem, weights_used.done((C0, E0)[n] + KT - 1))
                if n == 0 and t == 0:
                    dve.wait_ge(res_in, 16)
                for half in range(2):
                    if last_one and half == 1:
                        dve.wait_ge(weights_used.sem, weights_used.done(STEPS - 4))
                    part = xnat[:, t, half * HALF:(half + 1) * HALF]
                    nc.vector.scalar_tensor_tensor(out=part, in0=part, scalar=ALPHA, in1=ps[:, bank + half, :],
                                                   op0=ALU.mult, op1=ALU.add,
                                                   accum_out=sums[:, t, half:half + 1]).then_inc(res_done.sem, 1)
                dve.wait_ge(res_done.sem, res_done.done(2 * tile + 1))
                nc.vector.tensor_scalar(neg_mean[:, t:t + 1], sums[:, t, 0:1], sums[:, t, 1:2], -1.0 / D, ALU.add,
                                        ALU.mult).then_inc(ln_step.sem, 1)
                dve.wait_ge(ln_step.sem, ln_step.done(LN * tile))
                if t == 0:
                    dve.wait_ge(gb_in, 32 * (n + 1))
                row = xnat[:, t, :]
                nc.vector.scalar_tensor_tensor(out=scaled, in0=row, scalar=neg_mean[:, t:t + 1], in1=gb[:, 0, :],
                                               op0=ALU.add, op1=ALU.mult).then_inc(ln_step.sem, 1)
                if meanwhile:
                    meanwhile()
                dve.wait_ge(dev_full.sem, dev_full.done(tile))
                nc.vector.reciprocal(rstd[:, t:t + 1], dev[:, t:t + 1]).then_inc(ln_step.sem, 1)
                dve.wait_ge(ln_step.sem, ln_step.done(LN * tile + 2))
                for part in (slice(0, HALF), slice(HALF, D)) if last_one else (slice(0, D),):
                    nc.vector.scalar_tensor_tensor(out=row[:, part], in0=scaled[:, part], scalar=rstd[:, t:t + 1],
                                                   in1=gb[:, 1, part], op0=ALU.mult,
                                                   op1=ALU.add).then_inc(ln_step.sem, 1)

            for s in (w_lo, conv_step, pool_step, p_lo, lru_step, sconv_step, out_step, merge_step, h_full):
                dve.sem_inc(s.sem, s.credit)
            nc.vector.memset(eps[:], LN_EPS).then_inc(pads.sem, 1)
            for g, window in enumerate(POOL_WINDOWS):
                nc.vector.memset(inv_win[:, g:g + 1], 1.0 / window).then_inc(pads.sem, 1)
            dve.wait_ge(consts.sem, consts.done(1))
            nc.vector.reciprocal(tok1[:], tok1[:]).then_inc(corr_step.sem, 1)
            dve.wait_ge(corr_step.sem, corr_step.done(0))
            for g, window in enumerate(POOL_WINDOWS):
                nc.vector.tensor_scalar(corr[:, g, :], tok1[:], float(window), 1.0, ALU.mult,
                                        ALU.max).then_inc(corr_step.sem, 1)
            for t in range(TT):
                turned(2 * t, t, 2 * t, xT_h, xT_l)
                if t == 2:
                    dve.wait_ge(w_lo.sem, w_lo.done(A0))
                    split("A", 0, -2)
            split("A", 0, -1)
            dve.wait_ge(par_full.sem, par_full.done(0))
            nc.vector.tensor_copy(par[:, 0:DECAY, :].rearrange("p r k -> p (r k)"),
                                  ps[:, 7, 0:DECAY * KT]).then_inc(par_done.sem, 1)
            dve.wait_ge(par_done.sem, par_done.done(0))

            n_soft = [0]

            def soft_op(ins):
                ins.then_inc(soft_step.sem, 1)
                dve.wait_ge(soft_step.sem, soft_step.done(n_soft[0]))
                n_soft[0] += 1

            neg, z, den, f, f2, acc = (soft[:, n, :] for n in (0, 2, 3, 5, 6, 7))
            soft_op(nc.vector.tensor_scalar(neg, par[:, LAMBDA, :], -1.0, None, ALU.mult))
            soft_op(nc.vector.tensor_tensor(soft[:, 1, :], neg, par[:, LAMBDA, :], ALU.min))
            dve.wait_ge(soft_exp.sem, soft_exp.done(0))
            soft_op(nc.vector.tensor_scalar(den, z, 2.0, None, ALU.add))
            soft_op(nc.vector.reciprocal(soft[:, 4, :], den))
            soft_op(nc.vector.tensor_tensor(f, z, soft[:, 4, :], ALU.mult))
            soft_op(nc.vector.tensor_tensor(f2, f, f, ALU.mult))
            soft_op(nc.vector.tensor_scalar(acc, f2, 1.0 / 17, None, ALU.mult))
            for n in range(7, 0, -1):
                soft_op(nc.vector.scalar_tensor_tensor(out=acc, in0=acc, scalar=1.0 / (2 * n + 1), in1=f2,
                                                       op0=ALU.add, op1=ALU.mult))
            soft_op(nc.vector.scalar_tensor_tensor(out=acc, in0=acc, scalar=1.0, in1=f, op0=ALU.add, op1=ALU.mult))
            soft_op(nc.vector.tensor_scalar(neg, neg, 0.0, 4.0, ALU.max, ALU.mult))
            soft_op(nc.vector.scalar_tensor_tensor(out=par[:, DECAY, :], in0=acc, scalar=8.0, in1=neg,
                                                   op0=ALU.mult, op1=ALU.add))
            soft_op(nc.vector.tensor_scalar(par[:, DECAY_EXP, :], par[:, DECAY, :], -2.0, None, ALU.mult))
            for l in range(2):
                nc.vector.memset(u[l][:, 0:POOL_PAD], 0.0).then_inc(pads.sem, 1)
            nc.vector.memset(zl[:, 0:LRU_TAPS - 1], 0.0).then_inc(pads.sem, 1)
            nc.vector.memset(ch[:, 0:SCONV_TAPS - 1], 0.0).then_inc(pads.sem, 1)
            dve.wait_ge(pads.sem, pads.done(4 + GROUPS))
            dve.wait_ge(corr_step.sem, corr_step.done(GROUPS))

            def conv_taps(i, l):
                j = i * 2 + l
                dve.wait_ge(v_tap0.sem, v_tap0.done(j))
                for k in range(1, LRU_TAPS):
                    if k > 1:
                        dve.wait_ge(conv_step.sem, conv_step.done(j * CONV + (k - 2)))
                    nc.vector.scalar_tensor_tensor(out=v[:, l, :], in0=zl[:, k:k + SEQ],
                                                   scalar=cur[:, LRU_W0 + k, l:l + 1], in1=v[:, l, :],
                                                   op0=ALU.mult, op1=ALU.add).then_inc(conv_step.sem, 1)

            def v_low(i, l):
                dve.wait_ge(vr_hi.sem, vr_hi.done(i * 2 + l))
                nc.vector.tensor_tensor(vr_l[:, l, :], v[:, l, :], vr_h[:, l, :].bitcast(F32),
                                        ALU.subtract).then_inc(vr_lo.sem, 1)

            def pool_tile(i, l):
                j = i * 2 + l
                dve.wait_ge(pads.sem, pads.done(4 + GROUPS))
                dve.wait_ge(u_full.sem, u_full.done(j))
                dve.wait_ge(p_hi.sem, p_hi.done(j - 2))
                lag = u[l][:, bass.ds(lag_at, SEQ)]
                nc.vector.tensor_tensor_scan(ws[l], u[l][:, POOL_PAD:], lag, 0.0, ALU.add,
                                             ALU.subtract).then_inc(pool_step.sem, 1)
                dve.wait_ge(pool_step.sem, pool_step.done(j * POOL))
                nc.vector.tensor_tensor(ws[l][:, 0:POOL_PAD], ws[l][:, 0:POOL_PAD],
                                        corr[:, bass.ds(i, 1), :].rearrange("p g t -> p (g t)"),
                                        ALU.mult).then_inc(pool_step.sem, 1)
                dve.wait_ge(pool_step.sem, pool_step.done(j * POOL + 1))
                nc.vector.scalar_tensor_tensor(out=ws[l], in0=ws[l], scalar=inv_win[:, bass.ds(i, 1)],
                                               in1=u[l][:, POOL_PAD:], op0=ALU.mult,
                                               op1=ALU.subtract).then_inc(pool_step.sem, 1)

            def pool_low(i, l):
                dve.wait_ge(p_hi.sem, p_hi.done(i * 2 + l))
                nc.vector.tensor_tensor(p_l[:, l, :], ws[l], p_h[:, l, :].bitcast(F32),
                                        ALU.subtract).then_inc(p_lo.sem, 1)

            def lru_clamp(i):
                for l in range(2):
                    dve.wait_ge(t_full.sem, t_full.done(i * 2 + l))
                    nc.vector.tensor_scalar(sq[l], rt[l], TINY, None, ALU.max).then_inc(lru_step.sem, 1)

            def lru_rest(i):
                def after(n, l):
                    dve.wait_ge(lru_step.sem, lru_step.done(i * (2 * LRU) + (2 * n + l)))

                for l in range(2):
                    nc.vector.scalar_tensor_tensor(out=rt[l], in0=ae[l], scalar=1.0, in1=rt[l], op0=ALU.add,
                                                   op1=ALU.mult).then_inc(lru_step.sem, 1)
                for l in range(2):
                    after(1, l)
                    nc.vector.tensor_scalar(rt[l], rt[l], -1.0, 1.0, ALU.mult, ALU.add).then_inc(lru_step.sem, 1)
                for l in range(2):
                    dve.wait_ge(sq_full.sem, sq_full.done(i * 2 + l))
                    nc.vector.scalar_tensor_tensor(out=sq[l], in0=ae[l], scalar=1.0, in1=sq[l], op0=ALU.add,
                                                   op1=ALU.mult).then_inc(lru_step.sem, 1)
                for l in range(2):
                    dve.wait_ge(iv_done.sem, iv_done.done(i * 2 + l))
                    after(3, l)
                    nc.vector.tensor_tensor(sq[l], sq[l], ig[l], ALU.mult).then_inc(lru_step.sem, 1)
                h = ae
                for l in range(2):
                    after(4, l)
                    nc.vector.tensor_tensor_scan(h[l], rt[l], sq[l], 0.0, ALU.mult,
                                                 ALU.add).then_inc(lru_step.sem, 1)
                hi, lo = ([b[:, bass.ds(i * 2 + l, 1), :].rearrange("p k s -> p (k s)") for l in range(2)]
                          for b in (lru_h, lru_l))
                for l in range(2):
                    after(5, l)
                    nc.vector.tensor_scalar(hi[l], h[l], 1.0, None, ALU.mult).then_inc(lru_step.sem, 1)
                for l in range(2):
                    after(6, l)
                    nc.vector.tensor_tensor(lo[l], h[l], hi[l].bitcast(F32), ALU.subtract).then_inc(lru_step.sem, 1)

            def sconv(i, l):
                j = i * 2 + l
                dve.wait_ge(weights_used.sem, weights_used.done(step_no("A", i, 9)))
                dve.wait_ge(c_full.sem, c_full.done(j))
                dve.wait_ge(sconv_step.sem, sconv_step.done(j * SCONV - 1))
                nc.vector.scalar_tensor_tensor(out=ch[:, SCONV_TAPS - 1:], in0=ps[:, 4 + l, :],
                                               scalar=cur[:, B_H, l:l + 1], in1=c[:, l, :], op0=ALU.add,
                                               op1=ALU.mult).then_inc(sconv_step.sem, 1)
                dve.wait_ge(o_tap0.sem, o_tap0.done(j))
                for k in range(1, SCONV_TAPS):
                    if k > 1:
                        dve.wait_ge(sconv_step.sem, sconv_step.done(j * SCONV + (k - 1)))
                    nc.vector.scalar_tensor_tensor(out=o[:, l, :], in0=ch[:, k:k + SEQ],
                                                   scalar=cur[:, SC_W0 + k, l:l + 1], in1=o[:, l, :],
                                                   op0=ALU.mult, op1=ALU.add).then_inc(sconv_step.sem, 1)

            def conv_out(i, l):
                j = i * 2 + l
                if l == 0:
                    dve.wait_ge(weights_used.sem, weights_used.done(step_no("A", i, 11)))
                dve.wait_ge(sconv_step.sem, sconv_step.done(j * SCONV + 2))
                nc.vector.scalar_tensor_tensor(out=o[:, l, :], in0=ps[:, 6 + l, :], scalar=cur[:, B_B, l:l + 1],
                                               in1=o[:, l, :], op0=ALU.add, op1=ALU.mult).then_inc(out_step.sem, 1)
                hi, lo = (b[:, bass.ds(j, 1), :].rearrange("p k s -> p (k s)") for b in (cnv_h, cnv_l))
                dve.wait_ge(out_step.sem, out_step.done(j * OUT))
                nc.vector.tensor_scalar(hi, o[:, l, :], 1.0, None, ALU.mult).then_inc(out_step.sem, 1)
                dve.wait_ge(out_step.sem, out_step.done(j * OUT + 1))
                nc.vector.tensor_tensor(lo, o[:, l, :], hi.bitcast(F32), ALU.subtract).then_inc(out_step.sem, 1)

            split("A", 0, 0)
            with dve.Fori(0, A_ITERS) as i:
                lag_at = dve.snap(POOL_PAD - (POOL_WINDOWS[0] << i))
                nc.vector.tensor_scalar(cur[:], par[:, :, bass.ds(i * 2, 2)], 1.0, None,
                                        ALU.mult).then_inc(cur_set.sem, 1)
                dve.wait_ge(cur_set.sem, cur_set.done(i))
                for s in range(A_BODY):
                    if s:
                        split("A", i, s)
                    if s == 2:
                        conv_taps(i, 0)
                    if s == 3:
                        conv_taps(i, 1)
                        v_low(i, 0)
                    if s == 4:
                        v_low(i, 1)
                        for l in range(2):
                            pool_tile(i, l)
                        for l in range(2):
                            pool_low(i, l)
                    if s == 7:
                        for l in range(2):
                            if l == 0:
                                dve.wait_ge(weights_used.sem, weights_used.done(step_no("A", i, 6)))
                            nc.vector.tensor_scalar(
                                act32[:, bass.ds(i * 2 + l, 1), :].rearrange("p k s -> p (k s)"),
                                ps[:, 6 + l, :], cur[:, POOL_SCALE, l:l + 1], None, ALU.mult).then_inc(ypool.sem, 1)
                    if s == 8:
                        lru_clamp(i)
                    if s == 9:
                        lru_rest(i)
                    if s == 10:
                        sconv(i, 0)
                    if s == 11:
                        sconv(i, 1)
                split("A", i, A_BODY)
                for l in range(2):
                    conv_out(i, l)

            def b_pass(i, last=False):
                nc.vector.tensor_scalar(cur_b[:], par[:, B_GATE0:B_GATE2 + 1, bass.ds(i * 4, 4)], 1.0, None,
                                        ALU.mult).then_inc(cur_b_set.sem, 1)

                def merge(q, step):
                    for l in range(2):
                        g0, g1, g2 = (gates[:, m, l, :] for m in range(3))
                        y = act32[:, bass.ds(i * 4 + (2 * q + l), 1), :].rearrange("p k s -> p (k s)")
                        before = merge_step.done(i * 20 + merge_at(q, step - 1, l))
                        if step == 0:
                            dve.wait_ge(gate_full.sem, gate_full.done(i * 12 + (6 * q + l)))
                            args = (g0, g0, y, ALU.mult)
                        elif step == 1:
                            dve.wait_ge(gate_full.sem, gate_full.done(i * 12 + (6 * q + 2 + l)))
                            dve.wait_ge(weights_used.sem, weights_used.done(step_no("B", i, 10 * q + 7)))
                            args = (g1, g1, ps[:, (6, 0)[q] + l, :], ALU.mult)
                        elif step == 2:
                            dve.wait_ge(merge_step.sem, before)
                            args = (g0, g0, g1, ALU.add)
                        elif step == 3:
                            dve.wait_ge(gate_full.sem, gate_full.done(i * 12 + (6 * q + 4 + l)))
                            dve.wait_ge(weights_used.sem, weights_used.done(step_no("B", i, 10 * q + 9)))
                            args = (g2, g2, ps[:, (0, 2)[q] + l, :], ALU.mult)
                        else:
                            dve.wait_ge(merge_step.sem, before)
                            args = (y, g0, g2, ALU.add)
                        nc.vector.tensor_tensor(*args).then_inc(merge_step.sem, 1)

                for s in range(B_BODY):
                    if s:
                        split("B", i, s)
                    q, at = s // 10, s % 10
                    if at == 2:
                        merge(q, 0)
                    if at == 8:
                        merge(q, 1)
                        merge(q, 2)
                    if s == 10:
                        merge(0, 3)
                        merge(0, 4)
                if last:
                    for k in range(LOOKAHEAD):
                        stage(act32[:, k, :], k, k)
                else:
                    split("B", i, B_BODY)
                merge(1, 3)
                merge(1, 4)

            with dve.Fori(0, B_ITERS - 1) as i:
                b_pass(i)
            b_pass(B_ITERS - 1, last=True)

            for t in range(MT):
                turned(8 + 2 * t, t, 4 + 2 * t, memT_h, memT_l)
            for s in range(5):
                split("C", 0, s)
                k = s + LOOKAHEAD
                stage(act32[:, k, :], k, k % SPLIT_SLOTS)
            layer_norm(0, 0, 0)
            layer_norm(0, 1, 2)
            turned(12, 0, 0, xT_h, xT_l)
            layer_norm(0, 2, 4)
            turned(14, 1, 2, xT_h, xT_l)
            layer_norm(0, 3, 6)

            def maxima(h):
                for b in range(2):
                    dve.wait_ge(scores_full.sem, scores_full.done(2 * h + b))
                    nc.vector.tensor_reduce(row_max[:, 2 * b:2 * b + 2],
                                            ps[:, 6 + b, :].rearrange("p (t m) -> p t m", t=2),
                                            AX.X, ALU.max).then_inc(max_step.sem, 1)
                    dve.wait_ge(max_step.sem, max_step.done(4 * h + 2 * b))
                    nc.vector.tensor_scalar(neg_max[:, 2 * b:2 * b + 2], row_max[:, 2 * b:2 * b + 2],
                                            -SCORE_SCALE, None, ALU.mult).then_inc(max_step.sem, 1)

            def normalise(h):
                dve.wait_ge(exp_done.sem, exp_done.done(TT * h + TT - 1))
                nc.vector.reciprocal(inv_sum[:], row_sum[:]).then_inc(norm_step.sem, 1)
                dve.wait_ge(norm_step.sem, norm_step.done(5 * h))
                for t in range(TT):
                    nc.vector.tensor_scalar(probs[:, t, :], probs[:, t, :], inv_sum[:, t:t + 1], None,
                                            ALU.mult).then_inc(norm_step.sem, 1)

            def probs_low(h):
                for m in range(MT):
                    dve.wait_ge(pT_hi.sem, pT_hi.done(MT * h + m))
                    nc.vector.tensor_tensor(pT_l[:, m, :], ps[:, 6 + m, :], pT_h[:, m, :].bitcast(F32),
                                            ALU.subtract).then_inc(pT_lo.sem, 1)

            def weighed(h):
                for d in range(2):
                    dve.wait_ge(pv_full.sem, pv_full.done(2 * h + d))
                    nc.vector.tensor_copy(act32[:, 2 * h + d, :], ps[:, d, :]).then_inc(ot_full.sem, 1)

            for h in range(HEADS):
                base = HEAD_STEPS * h
                for s in range(HEAD_STEPS):
                    if h or s > 2:
                        split("D", 0, base + s)
                    if s == 2:
                        for d in range(2):
                            dve.wait_ge(kT_hi.sem, kT_hi.done(2 * h + d))
                            nc.vector.tensor_tensor(kT_l[:, d, :], ps[:, d, 0:M], kT_h[:, d, :].bitcast(F32),
                                                    ALU.subtract).then_inc(kT_lo.sem, 1)
                        if h == 0:
                            turned(16, 2, 4, xT_h, xT_l)
                            dve.wait_ge(w_lo.sem, w_lo.done(D0 + POOL_STEPS[-1]))
                            split("D", 0, 1)
                            split("D", 0, 2)
                            turned(18, 3, 6, xT_h, xT_l)
                    if s == 4:
                        for m in range(MT):
                            dve.wait_ge(v_hi.sem, v_hi.done(MT * h + m))
                            nc.vector.tensor_tensor(v_l[:, h % 2, m, :], ps[:, 2 + m, 0:HD],
                                                    v_h[:, h % 2, m, :].bitcast(F32),
                                                    ALU.subtract).then_inc(v_lo.sem, 1)
                        if h:
                            probs_low(h - 1)
                if h == HEADS - 1:
                    for k in range(4):
                        stage(act32[:, k, :], KT + k, k)
                for d in range(2):
                    dve.wait_ge(q_hi.sem, q_hi.done(2 * h + d))
                    nc.vector.tensor_tensor(qT_l[:, d, :], ps[:, 4 + d, :], qT_h[:, d, :].bitcast(F32),
                                            ALU.subtract).then_inc(q_lo.sem, 1)
                if h:
                    weighed(h - 1)
                if h == HEADS - 1:
                    split("E", 0, 0)
                maxima(h)
                normalise(h)
            probs_low(HEADS - 1)
            weighed(HEADS - 1)

            for s in range(1, 5):
                split("E", 0, s)
                k = s + LOOKAHEAD
                stage(act32[:, k, :], KT + k, k % SPLIT_SLOTS)
            layer_norm(1, 0, 2)
            layer_norm(1, 1, 4)
            turned(20, 0, 2, xT_h, xT_l)
            layer_norm(1, 2, 6, lambda: turned(22, 1, 4, xT_h, xT_l))
            layer_norm(1, 3, 0)
            turned(24, 2, 6, xT_h, xT_l)
            turned(26, 3, 0, xT_h, xT_l)

            def gate_and_up(i, first=0, stages=0, bank=2):
                for s in range(first, F_BODY):
                    split("F", i, s)
                for k in range(stages):
                    stage(hidden[:, k, :], 2 * KT + k, k)
                dve.wait_ge(weights_used.sem, weights_used.done(step_no("F", i, 3)))
                for l in range(2):
                    dve.wait_ge(silu_full.sem, silu_full.done(i * 2 + l))
                    nc.vector.tensor_tensor(hidden[:, bass.ds(i * 2 + l, 1), :].rearrange("p k s -> p (k s)"),
                                            silu[:, l, :], ps[:, bank + l, :], ALU.mult).then_inc(h_full.sem, 1)

            dve.wait_ge(w_lo.sem, w_lo.done(F0 + POOL_STEPS[-1]))
            gate_and_up(0, 1, bank=4)
            with dve.Fori(1, F_ITERS - 1) as i:
                gate_and_up(i)
            gate_and_up(F_ITERS - 1, 0, LOOKAHEAD)

            with dve.Fori(0, G_ITERS) as i:
                for s in range(G_BODY):
                    split("G", i, s)
                    k = s + LOOKAHEAD
                    stage(hidden[:, bass.ds(i * G_BODY + k, 1), :].rearrange("p k s -> p (k s)"),
                          i * G_BODY + (2 * KT + k), k % SPLIT_SLOTS)
            for s in range(G_ITERS * G_BODY, HT - LOOKAHEAD):
                split("G", 0, s)
                k = s + LOOKAHEAD
                stage(hidden[:, k, :], 2 * KT + k, k % SPLIT_SLOTS)
            for t in range(TT):
                layer_norm(2, t, 2 * t)


_INS = ["x", "mem", "w_in", "b_in", "pool_w", "pool_scale", "lru_conv_w", "lru_conv_b", "lru_w_r", "lru_b_r",
        "lru_w_i", "lru_b_i", "lru_lambda", "lru_w_out", "sconv_w", "sconv_w_out", "w_mix_out", "xa_w_q",
        "xa_w_k", "xa_w_v", "xa_w_o", "ffn_w_gate", "ffn_w_up", "ffn_w_down", "ln_g", "ln_b"]


def kernel(**inputs):
    import numpy as np
    import concourse.bacc as bacc
    from concourse.bass_utils import run_bass_kernel_spmd

    nc = bacc.Bacc("TRN2", target_bir_lowering=False, num_devices=1)
    arrays, args = {}, []
    for name in _INS:
        a = np.ascontiguousarray(inputs[name])
        arrays[f"in_{name}"] = a
        args.append(nc.dram_tensor(f"in_{name}", a.shape, mybir.dt.from_np(a.dtype), kind="ExternalInput").ap())
    out = nc.dram_tensor("out", arrays["in_x"].shape, F32, kind="ExternalOutput").ap()
    hybrid_layer(nc, *args, out)
    return run_bass_kernel_spmd(nc, [arrays], core_ids=[0]).results[0]["out"]
```
